# Optimizing a Trainium2 kernel written in Bass

```python
import math
import jax, jax.numpy as jnp
from jax import lax
import numpy as np

D_MODEL = 1024
BATCH = 1
SEQ = 256
DEPTH = 1

HEAD_DIM = 64
N_BRANCH = 4
BRANCH_WIDTH = D_MODEL // 2

SWA_HEADS = BRANCH_WIDTH // HEAD_DIM
SWA_KV_HEADS = SWA_HEADS // 4
SWA_WINDOW = 128
SWA_BLOCK = 128

CONV_CH = BRANCH_WIDTH
CONV_WIDTH = 31

FOX_HEADS = BRANCH_WIDTH // HEAD_DIM
FOX_QBLOCK = 128
FOX_FGATE_BIAS = 3.0

MOBA_HEADS = BRANCH_WIDTH // HEAD_DIM
MOBA_BLOCK = 256
MOBA_TOPK = 3
MOBA_QCHUNK = 128

D_FF = 2816
FFN_CONV_WIDTH = 3

REL_BUCKETS = 32
REL_MAX_DIST = 128
N_BIAS_HEADS = SWA_HEADS + MOBA_HEADS

EPS = 1e-6
NEG = -1e30

IN_SIZES = (
    SWA_HEADS * HEAD_DIM, SWA_KV_HEADS * HEAD_DIM, SWA_KV_HEADS * HEAD_DIM,
    2 * CONV_CH,
    FOX_HEADS * HEAD_DIM, FOX_HEADS * HEAD_DIM, FOX_HEADS * HEAD_DIM, FOX_HEADS,
    MOBA_HEADS * HEAD_DIM, MOBA_HEADS * HEAD_DIM, MOBA_HEADS * HEAD_DIM,
    N_BRANCH * D_MODEL,
)
D_IN = sum(IN_SIZES)
IN_SPLITS = tuple(int(s) for s in np.cumsum(IN_SIZES)[:-1])


def rmsnorm(x, g):
    x32 = x.astype(jnp.float32)
    y = x32 * lax.rsqrt(jnp.mean(x32 * x32, axis=-1, keepdims=True) + EPS)
    return (y * g.astype(jnp.float32)).astype(x.dtype)

def layernorm(x, g, b):
    x32 = x.astype(jnp.float32)
    mu = jnp.mean(x32, axis=-1, keepdims=True)
    xc = x32 - mu
    var = jnp.mean(xc * xc, axis=-1, keepdims=True)
    return (xc * lax.rsqrt(var + EPS) * g.astype(jnp.float32) + b.astype(jnp.float32)).astype(x.dtype)

def causal_depthwise_conv(x, w, b):
    k_width, ch = w.shape
    y = lax.conv_general_dilated(
        x, w[:, None, :].astype(x.dtype), window_strides=(1,), padding=[(k_width - 1, 0)],
        dimension_numbers=('NWC', 'WIO', 'NWC'), feature_group_count=ch)
    return y + b.astype(x.dtype)

def rel_bucket(dist):
    n = jnp.maximum(dist, 0)
    max_exact = REL_BUCKETS // 2
    nf = jnp.maximum(n, 1).astype(jnp.float32)
    large = max_exact + (jnp.log(nf / max_exact) / math.log(REL_MAX_DIST / max_exact)
                         * (REL_BUCKETS - max_exact)).astype(jnp.int32)
    large = jnp.minimum(large, REL_BUCKETS - 1)
    return jnp.where(n < max_exact, n, large)

def sliding_window_gqa(q, k, v, sinks, bias_tab):
    bsz, seq = q.shape[0], q.shape[1]
    nb = seq // SWA_BLOCK
    grp = SWA_HEADS // SWA_KV_HEADS
    qb = q.reshape(bsz, nb, SWA_BLOCK, SWA_KV_HEADS, grp, HEAD_DIM)
    kb = k.reshape(bsz, nb, SWA_BLOCK, SWA_KV_HEADS, HEAD_DIM)
    vb = v.reshape(bsz, nb, SWA_BLOCK, SWA_KV_HEADS, HEAD_DIM)
    shift = lambda t: jnp.concatenate([jnp.zeros_like(t[:, :1]), t[:, :-1]], axis=1)
    kk = jnp.concatenate([shift(kb), kb], axis=2)
    vv = jnp.concatenate([shift(vb), vb], axis=2)
    logits = jnp.einsum('bnqkgd,bnskd->bnkgqs', qb, kk).astype(jnp.float32) * (HEAD_DIM ** -0.5)
    qpos = jnp.arange(SWA_BLOCK) + SWA_BLOCK
    kpos = jnp.arange(2 * SWA_BLOCK)
    dist = qpos[:, None] - kpos[None, :]
    bias = bias_tab.astype(jnp.float32)[rel_bucket(dist)]
    bias = bias.transpose(2, 0, 1).reshape(SWA_KV_HEADS, grp, SWA_BLOCK, 2 * SWA_BLOCK)
    in_window = (dist >= 0) & (dist < SWA_WINDOW)
    has_prev = (jnp.arange(nb)[:, None] > 0) | (kpos[None, :] >= SWA_BLOCK)
    mask = in_window[None, :, :] & has_prev[:, None, :]
    logits = jnp.where(mask[None, :, None, None], logits + bias, NEG)
    sink = sinks.astype(jnp.float32).reshape(SWA_KV_HEADS, grp, 1, 1)
    m = jnp.maximum(jnp.max(logits, axis=-1, keepdims=True), sink)
    p = jnp.exp(logits - m)
    denom = jnp.sum(p, axis=-1, keepdims=True) + jnp.exp(sink - m)
    probs = (p / denom).astype(v.dtype)
    out = jnp.einsum('bnkgqs,bnskd->bnqkgd', probs, vv)
    return out.reshape(bsz, seq, SWA_HEADS * HEAD_DIM)

def conformer_conv(u, w_dw, b_dw, ln_g, ln_b):
    a, gt = jnp.split(u, 2, axis=-1)
    h = a * jax.nn.sigmoid(gt)
    h = causal_depthwise_conv(h, w_dw, b_dw)
    h = layernorm(h, ln_g, ln_b)
    return jax.nn.silu(h)

def forgetting_attention(q, k, v, f_logit, b_f):
    bsz, seq = q.shape[0], q.shape[1]
    nb = seq // FOX_QBLOCK
    q = q.reshape(bsz, seq, FOX_HEADS, HEAD_DIM)
    k = k.reshape(bsz, seq, FOX_HEADS, HEAD_DIM)
    v = v.reshape(bsz, seq, FOX_HEADS, HEAD_DIM)
    log_f = jax.nn.log_sigmoid(f_logit.astype(jnp.float32) + b_f.astype(jnp.float32))
    c = jnp.cumsum(log_f, axis=1).transpose(0, 2, 1)
    qb = q.reshape(bsz, nb, FOX_QBLOCK, FOX_HEADS, HEAD_DIM).transpose(1, 0, 2, 3, 4)
    cb = c.reshape(bsz, FOX_HEADS, nb, FOX_QBLOCK).transpose(2, 0, 1, 3)
    kpos = jnp.arange(seq)

    def block(args):
        qi, ci, i = args
        logits = jnp.einsum('bqhd,bshd->bhqs', qi, k).astype(jnp.float32) * (HEAD_DIM ** -0.5)
        logits = logits + ci[..., None] - c[:, :, None, :]
        qpos = i * FOX_QBLOCK + jnp.arange(FOX_QBLOCK)
        logits = jnp.where(kpos[None, :] <= qpos[:, None], logits, NEG)
        p = jax.nn.softmax(logits, axis=-1).astype(v.dtype)
        return jnp.einsum('bhqs,bshd->bqhd', p, v)

    out = lax.map(block, (qb, cb, jnp.arange(nb)))
    return out.transpose(1, 0, 2, 3, 4).reshape(bsz, seq, FOX_HEADS * HEAD_DIM)

def moba_attention(q, k, v, bias_tab):
    bsz, seq = q.shape[0], q.shape[1]
    nblk = -(-seq // MOBA_BLOCK)
    s_pad = nblk * MOBA_BLOCK
    padw = ((0, 0), (0, s_pad - seq), (0, 0), (0, 0))
    to_heads = lambda t: jnp.pad(t.reshape(bsz, seq, MOBA_HEADS, HEAD_DIM), padw).transpose(0, 2, 1, 3)
    q, k, v = to_heads(q), to_heads(k), to_heads(v)
    kb = k.reshape(bsz, MOBA_HEADS, nblk, MOBA_BLOCK, HEAD_DIM)
    vb = v.reshape(bsz, MOBA_HEADS, nblk, MOBA_BLOCK, HEAD_DIM)
    kmean = jnp.mean(kb.astype(jnp.float32), axis=3)
    gate = jnp.einsum('bhsd,bhnd->bhsn', q.astype(jnp.float32), kmean)
    qblk = jnp.arange(s_pad) // MOBA_BLOCK
    past = jnp.arange(nblk)[None, :] < qblk[:, None]
    gate = jnp.where(past, gate, NEG)
    n_sel = min(MOBA_TOPK, nblk)
    _, sel = lax.top_k(gate, n_sel)
    sel_valid = sel < qblk[None, None, :, None]
    bt = bias_tab.astype(jnp.float32).T
    bidx = jnp.arange(bsz)[:, None, None, None]
    hidx = jnp.arange(MOBA_HEADS)[None, :, None, None]
    hidx5 = jnp.arange(MOBA_HEADS)[None, :, None, None, None]
    scale = HEAD_DIM ** -0.5
    nq = s_pad // MOBA_QCHUNK

    def chunk(i):
        start = i * MOBA_QCHUNK
        qc = lax.dynamic_slice_in_dim(q, start, MOBA_QCHUNK, axis=2)
        selc = lax.dynamic_slice_in_dim(sel, start, MOBA_QCHUNK, axis=2)
        validc = lax.dynamic_slice_in_dim(sel_valid, start, MOBA_QCHUNK, axis=2)
        qpos = start + jnp.arange(MOBA_QCHUNK)
        kg = kb[bidx, hidx, selc]
        vg = vb[bidx, hidx, selc]
        kpos_g = selc[..., None] * MOBA_BLOCK + jnp.arange(MOBA_BLOCK)
        lg = jnp.einsum('bhqd,bhqnkd->bhqnk', qc, kg).astype(jnp.float32) * scale
        lg = lg + bt[hidx5, rel_bucket(qpos[None, None, :, None, None] - kpos_g)]
        lg = jnp.where(validc[..., None], lg, NEG).reshape(bsz, MOBA_HEADS, MOBA_QCHUNK, n_sel * MOBA_BLOCK)
        own = start // MOBA_BLOCK
        ko = lax.dynamic_slice_in_dim(k, own * MOBA_BLOCK, MOBA_BLOCK, axis=2)
        vo = lax.dynamic_slice_in_dim(v, own * MOBA_BLOCK, MOBA_BLOCK, axis=2)
        kpos_o = own * MOBA_BLOCK + jnp.arange(MOBA_BLOCK)
        dist_o = qpos[:, None] - kpos_o[None, :]
        lo = jnp.einsum('bhqd,bhsd->bhqs', qc, ko).astype(jnp.float32) * scale + bt[:, rel_bucket(dist_o)]
        lo = jnp.where(dist_o >= 0, lo, NEG)
        p = jax.nn.softmax(jnp.concatenate([lg, lo], axis=-1), axis=-1).astype(v.dtype)
        pg = p[..., :n_sel * MOBA_BLOCK].reshape(bsz, MOBA_HEADS, MOBA_QCHUNK, n_sel, MOBA_BLOCK)
        po = p[..., n_sel * MOBA_BLOCK:]
        return jnp.einsum('bhqnk,bhqnkd->bhqd', pg, vg) + jnp.einsum('bhqs,bhsd->bhqd', po, vo)

    out = lax.map(chunk, jnp.arange(nq))
    out = out.transpose(1, 0, 3, 2, 4).reshape(bsz, s_pad, MOBA_HEADS * HEAD_DIM)
    return out[:, :seq]

def hybrid_layer(x, ln1_g, w_in, b_gate, b_fgate, sinks, conv_w, conv_b, conv_ln_g, conv_ln_b,
                 w_br, w_out, ln2_g, w_up, ffn_conv_w, ffn_conv_b, w_down, rel_bias):
    bsz, seq = x.shape[0], x.shape[1]
    h = rmsnorm(x, ln1_g)
    z = h @ w_in
    (qa, ka, va, ub, qc, kc, vc, fc, qd, kd, vd, gz) = jnp.split(z, IN_SPLITS, axis=-1)
    gates = jax.nn.sigmoid(gz.reshape(bsz, seq, N_BRANCH, D_MODEL) + b_gate)
    ya = sliding_window_gqa(qa, ka, va, sinks, rel_bias[:, :SWA_HEADS])
    yb = conformer_conv(ub, conv_w, conv_b, conv_ln_g, conv_ln_b)
    yc = forgetting_attention(qc, kc, vc, fc, b_fgate)
    yd = moba_attention(qd, kd, vd, rel_bias[:, SWA_HEADS:])
    branches = jnp.stack([ya, yb, yc, yd], axis=2)
    proj = jnp.einsum('bsnc,ncd->bsnd', branches, w_br)
    merged = jnp.einsum('bsnd,bsnd->bsd', gates, proj)
    x = x + merged @ w_out
    h2 = rmsnorm(x, ln2_g)
    u = causal_depthwise_conv(h2 @ w_up, ffn_conv_w, ffn_conv_b)
    g_ff, v_ff = jnp.split(u, 2, axis=-1)
    return x + (jax.nn.silu(g_ff) * v_ff) @ w_down

def first_inputs(seed: int = 0) -> dict:
    key = jax.random.key(seed)
    ks = jax.random.split(key, 20)
    f32 = jnp.float32
    nrm = lambda kk, shape, s: jax.random.normal(kk, shape, f32) * s
    return {
        'x': nrm(ks[0], (BATCH, SEQ, D_MODEL), 1.0),
        'ln1_g': 1.0 + nrm(ks[1], (DEPTH, D_MODEL), 0.05),
        'w_in': nrm(ks[2], (DEPTH, D_MODEL, D_IN), D_MODEL ** -0.5),
        'b_gate': nrm(ks[3], (DEPTH, N_BRANCH, D_MODEL), 0.1),
        'b_fgate': FOX_FGATE_BIAS + nrm(ks[4], (DEPTH, FOX_HEADS), 0.1),
        'sinks': nrm(ks[5], (DEPTH, SWA_HEADS), 0.5),
        'conv_w': nrm(ks[6], (DEPTH, CONV_WIDTH, CONV_CH), CONV_WIDTH ** -0.5),
        'conv_b': nrm(ks[7], (DEPTH, CONV_CH), 0.02),
        'conv_ln_g': 1.0 + nrm(ks[8], (DEPTH, CONV_CH), 0.05),
        'conv_ln_b': nrm(ks[9], (DEPTH, CONV_CH), 0.02),
        'w_br': nrm(ks[10], (DEPTH, N_BRANCH, BRANCH_WIDTH, D_MODEL), BRANCH_WIDTH ** -0.5),
        'w_out': nrm(ks[11], (DEPTH, D_MODEL, D_MODEL), D_MODEL ** -0.5),
        'ln2_g': 1.0 + nrm(ks[12], (DEPTH, D_MODEL), 0.05),
        'w_up': nrm(ks[13], (DEPTH, D_MODEL, 2 * D_FF), D_MODEL ** -0.5),
        'ffn_conv_w': nrm(ks[14], (DEPTH, FFN_CONV_WIDTH, 2 * D_FF), FFN_CONV_WIDTH ** -0.5),
        'ffn_conv_b': nrm(ks[15], (DEPTH, 2 * D_FF), 0.02),
        'w_down': nrm(ks[16], (DEPTH, D_FF, D_MODEL), D_FF ** -0.5),
        'rel_bias': nrm(ks[17], (REL_BUCKETS, N_BIAS_HEADS), 0.5),
        'final_g': 1.0 + nrm(ks[18], (D_MODEL,), 0.05),
    }

def first_block(x, ln1_g, w_in, b_gate, b_fgate, sinks, conv_w, conv_b, conv_ln_g, conv_ln_b,
              w_br, w_out, ln2_g, w_up, ffn_conv_w, ffn_conv_b, w_down, rel_bias, final_g):
    for layer in range(DEPTH):
        x = hybrid_layer(x, ln1_g[layer], w_in[layer], b_gate[layer], b_fgate[layer], sinks[layer],
                         conv_w[layer], conv_b[layer], conv_ln_g[layer], conv_ln_b[layer],
                         w_br[layer], w_out[layer], ln2_g[layer], w_up[layer], ffn_conv_w[layer],
                         ffn_conv_b[layer], w_down[layer], rel_bias)
    return rmsnorm(x, final_g)


CHUNK = 64
Q_BLOCK = 128
NORM_EPS = 1e-5
POOL_WIDTH = D_MODEL // 2
POOL_WINDOWS = (2, 4, 8, 16)
POOL_GROUPS = len(POOL_WINDOWS)
POOL_GROUP_DIM = POOL_WIDTH // POOL_GROUPS
DIFF_HEADS = 4
DIFF_HEAD_DIM = 64
DIFF_V_DIM = 2 * DIFF_HEAD_DIM
DIFF_WIDTH = DIFF_HEADS * DIFF_V_DIM
QK_WIDTH = DIFF_HEADS * 2 * DIFF_HEAD_DIM
MIX_WIDTH = POOL_WIDTH + DIFF_WIDTH
IN_WIDTH = POOL_WIDTH + 2 * QK_WIDTH + DIFF_WIDTH
ROT_DIM = DIFF_HEAD_DIM // 4
ROPE_THETA = 500000.0
MEM_LEN = 256
X_HEADS = 4
X_HEAD_DIM = D_MODEL // X_HEADS
N_EXPERTS = 32
TOP_K = 4
D_EXPERT = D_MODEL
SWIGLU_ALPHA = 1.702
SWIGLU_LIMIT = 7.0
EXPERT_BLOCK = 128


def rms_norm(x, g):
    xf = x.astype(jnp.float32)
    y = xf * lax.rsqrt(jnp.mean(xf * xf, axis=-1, keepdims=True) + NORM_EPS)
    return (y * g.astype(jnp.float32)).astype(x.dtype)

def multiscale_pool(u, w_pool, pool_scale):
    B, S, _ = u.shape
    uf = u.astype(jnp.float32).reshape(B, S, POOL_GROUPS, POOL_GROUP_DIM)
    csum = jnp.pad(jnp.cumsum(uf, axis=1), ((0, 0), (1, 0), (0, 0), (0, 0)))
    t = jnp.arange(S)[:, None]
    win = jnp.array(POOL_WINDOWS, dtype=jnp.int32)[None, :]
    lo = jnp.maximum(t + 1 - win, 0)
    gidx = jnp.arange(POOL_GROUPS)[None, :]
    window_sum = csum[:, 1:] - csum[:, lo, gidx]
    count = (t + 1 - lo).astype(jnp.float32)
    mixed = (window_sum / count[None, :, :, None] - uf).astype(u.dtype)
    y = jnp.einsum('bsgc,gcd->bsgd', mixed, w_pool)
    y = y * pool_scale.reshape(POOL_GROUPS, POOL_GROUP_DIM)
    return y.reshape(B, S, POOL_WIDTH)

def rotary_tables(positions):
    inv_freq = ROPE_THETA ** (-jnp.arange(0, ROT_DIM, 2, dtype=jnp.float32) / ROT_DIM)
    ang = positions.astype(jnp.float32)[..., None] * inv_freq
    return jnp.cos(ang)[:, :, None, None, :], jnp.sin(ang)[:, :, None, None, :]

def partial_rotary(x, cos, sin):
    half = ROT_DIM // 2
    xr = x[..., :ROT_DIM].astype(jnp.float32)
    x1, x2 = xr[..., :half], xr[..., half:]
    rot = jnp.concatenate([x1 * cos - x2 * sin, x2 * cos + x1 * sin], axis=-1)
    return jnp.concatenate([rot.astype(x.dtype), x[..., ROT_DIM:]], axis=-1)

def diff_attention(q, k, v, lam):
    S = q.shape[3]
    scale = DIFF_HEAD_DIM ** -0.5
    outs = []
    for qb in range(S // Q_BLOCK):
        q0 = qb * Q_BLOCK
        kend = q0 + Q_BLOCK
        s = jnp.einsum('bhmqd,bhmkd->bhmqk', q[:, :, :, q0:kend], k[:, :, :, :kend],
                       preferred_element_type=jnp.float32) * scale
        q_chunk = (q0 + jnp.arange(Q_BLOCK)) // CHUNK
        k_chunk = jnp.arange(kend) // CHUNK
        mask = k_chunk[None, :] <= q_chunk[:, None]
        p = jax.nn.softmax(jnp.where(mask, s, -jnp.inf), axis=-1)
        a = p[:, :, 0] - lam * p[:, :, 1]
        outs.append(jnp.einsum('bhqk,bhkv->bhqv', a.astype(v.dtype), v[:, :, :kend]))
    return jnp.concatenate(outs, axis=2)

def cross_attention(h, mem_n, w_cq, w_ckv, w_co):
    B, S, _ = h.shape
    M = mem_n.shape[1]
    q = (h @ w_cq).reshape(B, S, X_HEADS, X_HEAD_DIM)
    kv = (mem_n @ w_ckv).reshape(B, M, 2, X_HEADS, X_HEAD_DIM)
    k, v = kv[:, :, 0], kv[:, :, 1]
    s = jnp.einsum('bshd,bmhd->bhsm', q, k, preferred_element_type=jnp.float32) * (X_HEAD_DIM ** -0.5)
    p = jax.nn.softmax(s, axis=-1)
    o = jnp.einsum('bhsm,bmhd->bshd', p.astype(v.dtype), v).reshape(B, S, D_MODEL)
    return o @ w_co

def clamped_swiglu(gu):
    gate, up = gu[..., :D_EXPERT], gu[..., D_EXPERT:]
    gate = jnp.minimum(gate, SWIGLU_LIMIT)
    up = jnp.clip(up, -SWIGLU_LIMIT, SWIGLU_LIMIT)
    return (up + 1.0) * gate * jax.nn.sigmoid(SWIGLU_ALPHA * gate)

def moe_ffn(h, w_router, b_router, w_gu, b_gu, w_down, b_down):
    B, S, D = h.shape
    T = B * S
    xt = h.reshape(T, D)
    logits = (xt @ w_router + b_router).astype(jnp.float32)
    top_val, top_idx = lax.top_k(logits, TOP_K)
    gates = jax.nn.softmax(top_val, axis=-1)
    flat_e = top_idx.reshape(-1)
    flat_tok = jnp.repeat(jnp.arange(T, dtype=jnp.int32), TOP_K)
    flat_g = gates.reshape(-1)
    order = jnp.argsort(flat_e)
    se = flat_e[order]
    counts = jnp.bincount(flat_e, length=N_EXPERTS)
    start = jnp.cumsum(counts) - counts
    pcounts = (counts + EXPERT_BLOCK - 1) // EXPERT_BLOCK * EXPERT_BLOCK
    pend = jnp.cumsum(pcounts)
    pstart = pend - pcounts
    dest = pstart[se] + jnp.arange(T * TOP_K) - start[se]
    n_rows = T * TOP_K + N_EXPERTS * EXPERT_BLOCK
    n_blocks = n_rows // EXPERT_BLOCK
    row_tok = jnp.zeros((n_rows,), jnp.int32).at[dest].set(flat_tok[order])
    row_gate = jnp.zeros((n_rows,), jnp.float32).at[dest].set(flat_g[order])
    block_e = jnp.minimum(jnp.searchsorted(pend, jnp.arange(n_blocks) * EXPERT_BLOCK, side='right'),
                          N_EXPERTS - 1)

    def expert_block(args):
        tok, g, e = args
        xb = xt[tok]
        hb = clamped_swiglu(xb @ w_gu[e] + b_gu[e])
        yb = hb @ w_down[e] + b_down[e]
        return yb * g[:, None].astype(yb.dtype)

    y_rows = lax.map(expert_block, (row_tok.reshape(n_blocks, EXPERT_BLOCK),
                                    row_gate.reshape(n_blocks, EXPERT_BLOCK), block_e))
    y = jnp.zeros((T, D), h.dtype).at[row_tok].add(y_rows.reshape(n_rows, D).astype(h.dtype))
    return y.reshape(B, S, D)

def second_inputs(seed: int = 0) -> dict:
    key = jax.random.key(seed)
    ks = jax.random.split(key, 32)
    f32 = jnp.float32
    L = DEPTH

    def nrm(k, shape, scale):
        return jax.random.normal(k, shape, f32) * scale

    def gain(k, shape):
        return 1.0 + 0.02 * jax.random.normal(k, shape, f32)

    offsets = jax.random.randint(ks[1], (BATCH, 1), 0, 4096, dtype=jnp.int32)
    return {
        'x': nrm(ks[0], (BATCH, SEQ, D_MODEL), 1.0),
        'positions': offsets + jnp.arange(SEQ, dtype=jnp.int32)[None, :],
        'mem': nrm(ks[2], (BATCH, MEM_LEN, D_MODEL), 1.0),
        'attn_norm_g': gain(ks[3], (L, D_MODEL)),
        'w_in': nrm(ks[4], (L, D_MODEL, IN_WIDTH), D_MODEL ** -0.5),
        'w_pool': nrm(ks[5], (L, POOL_GROUPS, POOL_GROUP_DIM, POOL_GROUP_DIM), POOL_GROUP_DIM ** -0.5),
        'pool_scale': gain(ks[6], (L, POOL_WIDTH)),
        'lambda_q1': nrm(ks[7], (L, DIFF_HEAD_DIM), 0.1),
        'lambda_k1': nrm(ks[8], (L, DIFF_HEAD_DIM), 0.1),
        'lambda_q2': nrm(ks[9], (L, DIFF_HEAD_DIM), 0.1),
        'lambda_k2': nrm(ks[10], (L, DIFF_HEAD_DIM), 0.1),
        'subln_g': gain(ks[11], (L, DIFF_V_DIM)),
        'w_out': nrm(ks[12], (L, MIX_WIDTH, D_MODEL), MIX_WIDTH ** -0.5),
        'xattn_norm_g': gain(ks[13], (L, D_MODEL)),
        'mem_norm_g': gain(ks[14], (L, D_MODEL)),
        'w_cq': nrm(ks[15], (L, D_MODEL, D_MODEL), D_MODEL ** -0.5),
        'w_ckv': nrm(ks[16], (L, D_MODEL, 2 * D_MODEL), D_MODEL ** -0.5),
        'w_co': nrm(ks[17], (L, D_MODEL, D_MODEL), D_MODEL ** -0.5),
        'ffn_norm_g': gain(ks[18], (L, D_MODEL)),
        'w_router': nrm(ks[19], (L, D_MODEL, N_EXPERTS), D_MODEL ** -0.5),
        'b_router': nrm(ks[20], (L, N_EXPERTS), 0.01),
        'w_gu': nrm(ks[21], (L, N_EXPERTS, D_MODEL, 2 * D_EXPERT), D_MODEL ** -0.5),
        'b_gu': nrm(ks[22], (L, N_EXPERTS, 2 * D_EXPERT), 0.01),
        'w_down': nrm(ks[23], (L, N_EXPERTS, D_EXPERT, D_MODEL), D_EXPERT ** -0.5),
        'b_down': nrm(ks[24], (L, N_EXPERTS, D_MODEL), 0.01),
        'final_norm_g': gain(ks[25], (D_MODEL,)),
    }

def second_block(x, positions, mem, attn_norm_g, w_in, w_pool, pool_scale, lambda_q1, lambda_k1,
              lambda_q2, lambda_k2, subln_g, w_out, xattn_norm_g, mem_norm_g, w_cq, w_ckv, w_co,
              ffn_norm_g, w_router, b_router, w_gu, b_gu, w_down, b_down, final_norm_g):
    B, S, _ = x.shape
    cos, sin = rotary_tables(positions)
    for l in range(DEPTH):
        h = rms_norm(x, attn_norm_g[l])
        u = h @ w_in[l]
        u_pool, u_q, u_k, u_v = jnp.split(
            u, [POOL_WIDTH, POOL_WIDTH + QK_WIDTH, POOL_WIDTH + 2 * QK_WIDTH], axis=-1)
        y_pool = multiscale_pool(u_pool, w_pool[l], pool_scale[l])

        q = partial_rotary(u_q.reshape(B, S, DIFF_HEADS, 2, DIFF_HEAD_DIM), cos, sin)
        k = partial_rotary(u_k.reshape(B, S, DIFF_HEADS, 2, DIFF_HEAD_DIM), cos, sin)
        q = q.transpose(0, 2, 3, 1, 4)
        k = k.transpose(0, 2, 3, 1, 4)
        v = u_v.reshape(B, S, DIFF_HEADS, DIFF_V_DIM).transpose(0, 2, 1, 3)
        lam_init = 0.8 - 0.6 * math.exp(-0.3 * l)
        lam = (jnp.exp(jnp.sum(lambda_q1[l].astype(jnp.float32) * lambda_k1[l].astype(jnp.float32)))
               - jnp.exp(jnp.sum(lambda_q2[l].astype(jnp.float32) * lambda_k2[l].astype(jnp.float32)))
               + lam_init)
        o = diff_attention(q, k, v, lam)
        o = rms_norm(o, subln_g[l]) * (1.0 - lam_init)
        y_diff = o.transpose(0, 2, 1, 3).reshape(B, S, DIFF_WIDTH)
        x = x + jnp.concatenate([y_pool, y_diff], axis=-1) @ w_out[l]

        x = x + cross_attention(rms_norm(x, xattn_norm_g[l]), rms_norm(mem, mem_norm_g[l]),
                                w_cq[l], w_ckv[l], w_co[l])

        x = x + moe_ffn(rms_norm(x, ffn_norm_g[l]), w_router[l], b_router[l], w_gu[l], b_gu[l],
                        w_down[l], b_down[l])
    return rms_norm(x, final_norm_g)


def setup_inputs(seed=0):
    out = dict(first_inputs(seed))
    for name, value in second_inputs(seed + 1).items():
        if name != "x":
            out[name + "_2"] = value
    return out


def reference(
    x, ln1_g, w_in, b_gate, b_fgate, sinks, conv_w, conv_b, conv_ln_g, conv_ln_b, w_br, w_out,
    ln2_g, w_up, ffn_conv_w, ffn_conv_b, w_down, rel_bias, final_g, positions_2, mem_2,
    attn_norm_g_2, w_in_2, w_pool_2, pool_scale_2, lambda_q1_2, lambda_k1_2, lambda_q2_2,
    lambda_k2_2, subln_g_2, w_out_2, xattn_norm_g_2, mem_norm_g_2, w_cq_2, w_ckv_2, w_co_2,
    ffn_norm_g_2, w_router_2, b_router_2, w_gu_2, b_gu_2, w_down_2, b_down_2, final_norm_g_2,
):
    x = first_block(
        x, ln1_g, w_in, b_gate, b_fgate, sinks, conv_w, conv_b, conv_ln_g, conv_ln_b, w_br,
        w_out, ln2_g, w_up, ffn_conv_w, ffn_conv_b, w_down, rel_bias, final_g,
    )
    return second_block(
        x, positions_2, mem_2, attn_norm_g_2, w_in_2, w_pool_2, pool_scale_2, lambda_q1_2,
        lambda_k1_2, lambda_q2_2, lambda_k2_2, subln_g_2, w_out_2, xattn_norm_g_2, mem_norm_g_2,
        w_cq_2, w_ckv_2, w_co_2, ffn_norm_g_2, w_router_2, b_router_2, w_gu_2, b_gu_2, w_down_2,
        b_down_2, final_norm_g_2,
    )


_drawn_inputs = setup_inputs


def setup_inputs(seed=0):
    import zlib

    import numpy as np

    out = dict(_drawn_inputs(seed))
    spreads = {}
    factors = {'sinks': 3.907,
     'lambda_k2_2': 3.256,
     'xattn_norm_g_2': 5.12,
     'mem_norm_g_2': 5.295,
     'b_gu_2': 47.185,
     'b_down_2': 54.216,
     'final_norm_g_2': 7.928,
     'ffn_norm_g_2': 6.332,
     'b_router_2': 8.0}
    for name, (base, spread) in spreads.items():
        noise = np.random.default_rng([zlib.crc32(name.encode()), seed]).standard_normal(out[name].shape)
        drawn = base * np.exp(spread * noise) if base else spread * noise
        out[name] = __import__('jax').numpy.asarray(drawn.astype(out[name].dtype))
    for name, factor in factors.items():
        out[name] = (out[name] * factor).astype(out[name].dtype)
    return out
```

```python
import math
from contextlib import ExitStack

import concourse.bass as bass
import numpy as np
from concourse import mybir

F32 = mybir.dt.float32
I32 = mybir.dt.int32
ALU = mybir.AluOpType
ACT = mybir.ActivationFunctionType
AX = mybir.AxisListType

P = 128
S = 256
TT = S // P
D = 1024
KT = D // P
BR = D // 2
BT = BR // P
HD = 64
SWA_H, KV_H = 8, 2
SWA_WINDOW = 128
FOX_H = MOBA_H = 8
CONV_W = 31
D_FF = 2816
FT = D_FF // P
BUCKETS, MAX_DIST = 32, 128
BIAS_H = SWA_H + MOBA_H
EPS1, EPS2 = 1e-6, 1e-5
NEG = -1e30
DIFF_H, DIFF_V = 4, 128
CHUNK = 64
ROT, THETA = 16, 500000.0
LAM_INIT = 0.8 - 0.6 * math.exp(-0.3 * 0)
X_H, X_HD = 4, 256
POOL_W = (2, 4, 8, 16)
NE, TOPK = 32, 4
ALPHA, LIMIT = 1.702, 7.0
CAP = 64
OVER = S * TOPK // (CAP + 1)
TOEP = 384

SIZES = dict(qa=512, ka=128, va=128, ub=1024, qc=512, kc=512, vc=512, fc=8, qd=512, kd=512, vd=512, gz=4 * D)
OFF, _at = {}, 0
for _n, _s in SIZES.items():
    OFF[_n] = _at
    _at += _s

SLOT = 2048
RING = 6
AREAS = 31620
SMALL = 1700


def shape_constants():
    i = np.arange(P)
    parts = {}
    parts["ident"] = np.eye(P)
    parts["flip"] = np.eye(P)[::-1]
    parts["tri"] = (i[:, None] < i[None, :])
    parts["ones"] = np.ones((P, P))
    rot = np.zeros((P, P))
    half = ROT // 2
    for head in range(P // HD):
        for d in range(half):
            rot[head * HD + half + d, head * HD + d] = -1.0
            rot[head * HD + d, head * HD + half + d] = 1.0
    parts["rot"] = rot
    freq = np.zeros((P, 1))
    base = (np.float32(THETA) ** (-np.arange(0, ROT, 2, dtype=np.float32) / np.float32(ROT))).astype(np.float32)
    for p in range(P):
        if p % HD < ROT:
            freq[p, 0] = base[(p % HD) % half]
    parts["freq"] = freq
    parts["iota2"] = np.tile(np.arange(CAP), (P, 2))
    parts["part"] = i[:, None]
    q, k = P + i[:, None], np.arange(S)[None, :]
    parts["causal"] = np.where(k <= q, 0.0, NEG)
    parts["chunk1"] = np.where(k // CHUNK <= q // CHUNK, 0.0, NEG)
    inv = np.zeros((P, 4 * 16))
    for g, w in enumerate(POOL_W):
        inv[:, g * 16:(g + 1) * 16] = 1.0 / np.minimum(np.arange(16) + 1, w)
    parts["invc"] = inv
    m = np.arange(TOEP)
    dist = 2 * P - 1 - m
    n = np.maximum(dist, 0)
    exact = BUCKETS // 2
    nf = np.maximum(n, 1).astype(np.float32)
    large = exact + (np.log(nf / np.float32(exact)) / np.float32(math.log(MAX_DIST / exact))
                     * np.float32(BUCKETS - exact)).astype(np.int32)
    bucket = np.where(n < exact, n, np.minimum(large, BUCKETS - 1))
    for name, ok in (("diag_swa", (dist >= 0) & (dist < SWA_WINDOW)), ("diag_moba", dist >= 0)):
        e = np.zeros((P, TOEP))
        e[bucket[ok], m[ok]] = 1.0
        e[BUCKETS, ~ok] = NEG
        parts[name] = e
    where, at = {}, 0
    for name, a in parts.items():
        where[name] = (at, a.shape[1])
        at += a.shape[1]
    return np.concatenate([np.asarray(a, np.float32) for a in parts.values()], axis=1), where


class Signal:

    def __init__(self, handle):
        self.handle, self.count = handle, 0


def tokens(after):
    if isinstance(after, tuple) and after and isinstance(after[0], Signal):
        return [after]
    return [t for a in after for t in tokens(a)]


class Queue:

    def __init__(self, done):
        self.done, self.items, self.seen = done, [], {}

    def waits(self, after):
        need = {}
        for s, v in tokens(after):
            if self.seen.get(s, 0) < v:
                need[s] = max(need.get(s, 0), v)
        self.seen.update(need)
        return [(s.handle, v) for s, v in need.items()]

    def __call__(self, emit, after=()):
        self.done.count += 1
        self.items.append((self.waits(after), emit, self.done.handle, 1))
        return (self.done, self.done.count)

    def matmuls(self, products, after=()):
        for n, (out, lhs, rhs, start, stop, own) in enumerate(products):
            def emit(e, out=out, lhs=lhs, rhs=rhs, start=start, stop=stop):
                return e.matmul(out, lhs, rhs, start=start, stop=stop, skip_group_check=True)
            waits = self.waits([after if n == 0 else (), own])
            last = n == len(products) - 1
            self.items.append((waits, emit, self.done.handle if last else None, 1))
        self.done.count += 1
        return (self.done, self.done.count)

    def transposes(self, pairs, ident, after=()):
        for n, (out, src) in enumerate(pairs):
            def emit(e, out=out, src=src):
                return e.transpose(out, src, ident)
            last = n == len(pairs) - 1
            self.items.append((self.waits(after if n == 0 else ()), emit, self.done.handle if last else None, 1))
        self.done.count += 1
        return (self.done, self.done.count)

    def load(self, signal, transfers, after=()):
        for n, (dst, src) in enumerate(transfers):
            def emit(e, dst=dst, src=src):
                return e.dma_start(dst, src(e) if callable(src) else src)
            self.items.append((self.waits(after if n == 0 else ()), emit, signal.handle, 16))
            signal.count += 16
        return (signal, signal.count)


class Buffer:
    def __init__(self, ap, signal=None):
        self.ap, self.landed, self.free, self.held = ap, signal, [], False


class Pool:

    def __init__(self, buffers):
        self.idle = list(buffers)

    def take(self):
        b = self.idle.pop(0)
        assert not b.held
        b.held = True
        return b

    def release(self, b, readers):
        b.free, b.held = [readers], False
        self.idle.append(b)


def interleave(*stages):
    live = [iter(s) for s in stages]
    while live:
        for s in list(live):
            try:
                next(s)
            except StopIteration:
                live.remove(s)


def hybrid_moe_program(nc, a, out, const_cols, stop=None):
    ctx = ExitStack()
    with ctx:
        def sem(name):
            return Signal(ctx.enter_context(nc.semaphore(name)))

        def sb(name, n, parts=P, dt=F32):
            return ctx.enter_context(nc.sbuf_tensor(name, [parts, n], dt))

        n_const = sum(w for _, w in const_cols.values())
        const_sb = sb("const_sb", n_const)
        cols_sb = sb("cols_sb", 4 * P)
        x_sb = sb("x_sb", KT * S)
        h_sb = sb("h_sb", KT * S)
        rstd_sb = sb("rstd_sb", 2 * S)
        small_sb = sb("small_sb", SMALL)
        arena_n = AREAS + RING * SLOT
        arena = sb("arena", arena_n)
        flag_sb = ctx.enter_context(nc.sbuf_tensor("flag_sb", [P, 32], I32))
        pos_i = ctx.enter_context(nc.sbuf_tensor("pos_i", [P, S], I32))
        bank_t = [ctx.enter_context(nc.psum_tensor(f"bank{i}", [P, 512], F32)) for i in range(8)]
        banks = Pool([Buffer(t) for t in bank_t])
        diag_dram = nc.dram_tensor("diag_dram", (BIAS_H, TOEP), F32).ap()

        def C(name, p0=0, p1=P):
            at, w = const_cols[name]
            return const_sb[p0:p1, at:at + w]

        ident, ones = C("ident"), C("ones")

        pe, act, dve, pool = (Queue(sem(n)) for n in ("pe_done", "act_done", "dve_done", "pool_done"))
        sp = Queue(sem("sp_unused"))

        def fence():
            return [(q.done, q.done.count) for q in (pe, act, dve, pool) if q.done.count]

        def tt(o, x, y, op, after=()):
            return dve(lambda e: e.tensor_tensor(o, x, y, op), after)

        def ts(o, x, s1, op1, s2=None, op2=None, after=()):
            if op2 is None:
                return dve(lambda e: e.tensor_scalar(o, x, s1, None, op1), after)
            return dve(lambda e: e.tensor_scalar(o, x, s1, s2, op1, op2), after)

        def stt(o, x, s, y, op1, op2, after=()):
            return dve(lambda e: e.scalar_tensor_tensor(out=o, in0=x, scalar=s, in1=y, op0=op1, op1=op2), after)

        def af(o, x, f, after=(), **k):
            return act(lambda e: e.activation(o, x, f, **k), after)

        def recip(o, x, after=()):
            return dve(lambda e: e.reciprocal(o, x), after)

        def neg_max(o, x, after=()):
            return dve(lambda e: e.tensor_reduce(o, x, AX.X, ALU.max, negate=True), after)

        def evac(o, x, after, on):
            if on is act:
                return af(o, x, ACT.Copy, after)
            return dve(lambda e: e.tensor_copy(o, x), after)

        free_at = [0]

        def area(n, *dims):
            at = free_at[0]
            free_at[0] += n
            assert free_at[0] <= AREAS, free_at[0]
            return arena[:, at:at + n]

        def tiles(ap, n):
            return ap.rearrange("p (n s) -> p n s", n=n)

        ring = Pool([Buffer(arena[:, arena_n - (i + 1) * SLOT:arena_n - i * SLOT], sem(f"slot{i}_loaded"))
                     for i in range(RING)])

        def unit(transfers):
            b = ring.take()
            b.token = sp.load(b.landed, [(v(b.ap), src) for v, src in transfers], after=b.free)
            return b

        def columns(w, c0, n=256):
            return unit([(lambda s: s[:, 0:KT * n].rearrange("p (k n) -> p k n", k=KT),
                          w[:, c0:c0 + n].rearrange("(k p) n -> p k n", p=P))])

        def small_load(name, dst, src, queue=act, after=()):
            return queue.load(sem(name), [(dst, src)], after)

        x = tiles(x_sb[:, :], KT)
        h = tiles(h_sb[:, :], KT)
        xin = area(2 * D).rearrange("p (t d) -> p t d", t=TT)
        x_loaded = small_load("x_loaded", xin, a["x"][0].rearrange("(t p) d -> p t d", p=P))
        const_loaded = small_load("const_loaded", const_sb[:, :], a["consts"])

        rows_in = [
            [("ln1_g", a["ln1_g"][0], 8), ("b_gate", a["b_gate"][0], 32), ("conv_b", a["conv_b"][0], 4),
             ("conv_ln_g", a["conv_ln_g"][0], 4), ("conv_ln_b", a["conv_ln_b"][0], 4), ("ln2_g", a["ln2_g"][0], 8),
             ("ffn_b", a["ffn_conv_b"][0], 44), ("final_g", a["final_g"], 8)],
            [("tap0", a["ffn_conv_w"][0, 0], 44), ("tap1", a["ffn_conv_w"][0, 1], 44),
             ("attn_g", a["attn_norm_g_2"][0], 8), ("xattn_g", a["xattn_norm_g_2"][0], 8),
             ("mem_g", a["mem_norm_g_2"][0], 8), ("ffn_g", a["ffn_norm_g_2"][0], 8)],
            [("tap2", a["ffn_conv_w"][0, 2], 44), ("pool_scale", a["pool_scale_2"][0], 4),
             ("subln", a["subln_g_2"][0], 1)],
            [("conv_w", a["conv_w"][0], CONV_W * BT)],
        ]
        rows_sb = area(4 * P)
        col_at, rows_loaded = {}, []
        for t, group in enumerate(rows_in):
            r = 0
            s = sem(f"rows{t}_loaded")
            for name, src, n in group:
                flat = src if len(src.shape) == 1 else src.rearrange("a b -> (a b)")
                token = act.load(s, [(rows_sb[r:r + n, t * P:(t + 1) * P], flat.rearrange("(r p) -> r p", p=P))])
                col_at[name] = t * P + r
                r += n
            rows_loaded.append((token, r))

        def col(name, i=0):
            return cols_sb[:, col_at[name] + i:col_at[name] + i + 1]

        sm_at = [0]

        def small(n, p1=P):
            at = sm_at[0]
            sm_at[0] += n
            assert sm_at[0] <= SMALL
            return small_sb[0:p1, at:at + n]

        relb = small(BIAS_H, BUCKETS + 1)
        relb_ones = dve(lambda e: e.memset(relb, 1.0))
        relb_loaded = small_load("relb_loaded", relb[0:BUCKETS, :], a["rel_bias"], after=relb_ones)
        bfg = small(1, FOX_H)
        bfg_loaded = small_load("bfg_loaded", bfg, a["b_fgate"][0].rearrange("(h o) -> h o", o=1))
        sinks = small(SWA_H)
        sinks_loaded = small_load("sinks_loaded", sinks, a["sinks"][0:1, :].broadcast_to([P, SWA_H]))
        wfc = small(KT * FOX_H).rearrange("p (k n) -> p k n", k=KT)
        w_in = a["w_in"][0]
        wfc_loaded = small_load("wfc_loaded", wfc,
                                w_in[:, OFF["fc"]:OFF["fc"] + FOX_H].rearrange("(k p) n -> p k n", p=P))
        lams = small(4 * HD)
        lam_sem = sem("lam_loaded")
        for i, n in enumerate(("lambda_q1_2", "lambda_k1_2", "lambda_q2_2", "lambda_k2_2")):
            lam_loaded = act.load(lam_sem, [(lams[:, i * HD:(i + 1) * HD], a[n][0:1, :].broadcast_to([P, HD]))])
        wrt = small(KT * NE).rearrange("p (k n) -> p k n", k=KT)
        wrt_loaded = small_load("wrt_loaded", wrt, a["w_router_2"][0].rearrange("(k p) n -> p k n", p=P))
        brt = small(NE)
        brt_loaded = small_load("brt_loaded", brt, a["b_router_2"][0:1, :].broadcast_to([P, NE]))
        pos_loaded = small_load("pos_loaded", pos_i[:, :], a["positions_2"][0:1, :].broadcast_to([P, S]))

        b = banks.take()
        for t, (token, r) in enumerate(rows_loaded):
            done = pe.transposes([(b.ap[:, t * P:t * P + r], rows_sb[0:r, t * P:(t + 1) * P])], ident[0:r, 0:r],
                                 after=[token, const_loaded])
        cols_ready = []
        for t, (_, r) in enumerate(rows_loaded):
            cols_ready.append(evac(cols_sb[:, t * P:t * P + r], b.ap[:, t * P:t * P + r], done, dve))
        banks.release(b, cols_ready)
        cw0 = col_at["conv_w"]
        taps_ready = ts(cols_sb[:, cw0:cw0 + CONV_W * BT], cols_sb[:, cw0:cw0 + CONV_W * BT], 0.5, ALU.mult,
                        after=cols_ready)

        def turn(dst, src, ready):
            got = []
            for k in range(0, KT, 2):
                b = banks.take()
                done = pe.transposes([(b.ap[:, j * S + t * P:j * S + (t + 1) * P], src[:, t, (k + j) * P:(k + j + 1) * P])
                                      for j in range(2) for t in range(TT)], ident, after=[ready, const_loaded, b.free])
                got.append(evac(dst[:, k:k + 2, :], b.ap[:, :].rearrange("p (n s) -> p n s", n=2), done,
                                act if k % 4 else dve))
                banks.release(b, got[-1])
            return [got[k // 2] for k in range(KT)]

        def inverse_root(total, n, eps, done, dst):
            r = ts(dst, total, 1.0 / n, ALU.mult, eps, ALU.add, after=done)
            r = recip(dst, dst, r)
            return af(dst, dst, ACT.Sqrt, r)

        def rms(src, ready, gain, eps, dst, dst_free=()):
            b = banks.take()
            half = KT // 2
            sq1 = af(dst[:, 0:half, :], src[:, 0:half, :], ACT.Square, [ready[0:half], dst_free])
            sq2 = tt(dst[:, half:KT, :], src[:, half:KT, :], src[:, half:KT, :], ALU.mult, [ready, dst_free])
            total = b.ap[:, 0:S]
            done = pe.matmuls([(total, ones, dst[:, k, :], k == 0, k == KT - 1, sq1 if k < half else sq2)
                               for k in range(KT)], after=[b.free, const_loaded])
            root = inverse_root(total, D, eps, [done, rstd_free[0]], rstd_sb[:, 0:S])
            banks.release(b, root)
            got = [stt(dst[:, k, :], src[:, k, :], col(gain, k), rstd_sb[:, 0:S], ALU.mult, ALU.mult,
                       [root, cols_ready]) for k in range(KT)]
            rstd_free[0] = got[-1]
            return got

        rstd_free = [()]

        def project(u, act_in, ready, take, n=2):
            w = u.ap[:, 0:KT * n * P].rearrange("p (k n) -> p k n", k=KT)
            b = banks.take()
            prods = []
            for j in range(n):
                for k in range(KT):
                    prods.append((b.ap[:, j * S:(j + 1) * S], w[:, k, j * P:(j + 1) * P], act_in[:, k, :], k == 0, k == KT - 1, ready[k]))
            done = pe.matmuls(prods, after=[b.free, u.token])
            ring.release(u, done)
            banks.release(b, take(b.ap[:, 0:n * S].rearrange("p (n s) -> p n s", n=n), done))

        def project_tokens(u, act_in, ready, take, n=256):
            w = u.ap[:, 0:KT * n].rearrange("p (k n) -> p k n", k=KT)
            b = banks.take()
            done = pe.matmuls([(b.ap[:, t * n:(t + 1) * n], act_in[:, k, t * P:(t + 1) * P], w[:, k, :],
                                k == 0, k == KT - 1, ready[k]) for t in range(TT) for k in range(KT)],
                              after=[b.free, u.token])
            ring.release(u, done)
            banks.release(b, take(b.ap[:, 0:TT * n].rearrange("p (t n) -> p t n", t=TT), done))

        x_ready = turn(x, xin, x_loaded)
        h_ready = rms(x, x_ready, "ln1_g", EPS1, h)
        cut_at = fence()

        yt = tiles(area(16 * S), 16)
        gate_a = area(32 * S)
        gate = tiles(gate_a, 32)
        qkv0 = free_at[0]
        qa, qc, kc, qd, kd = (tiles(area(BT * S), BT) for _ in range(5))
        ka = area(S)
        va = area(TT * 128).rearrange("p (t n) -> p t n", t=TT)
        vc, vd = (area(TT * BR).rearrange("p (t n) -> p t n", t=TT) for _ in range(2))
        toep_a = xin.rearrange("p t d -> p (t d)")
        scores = [Buffer(area(384)) for _ in range(3)]
        probs = [Buffer(area(384)) for _ in range(3)]
        score_pool, prob_pool = Pool(scores), Pool(probs)
        fox_l = area(FOX_H * S)
        fox_rt = area(FOX_H * S)

        diag_sb = small(TOEP, BIAS_H)
        b, b2 = banks.take(), banks.take()
        relb_swa = relb[:, 0:SWA_H]
        done = pe.matmuls([(b.ap[0:SWA_H, 0:TOEP], relb_swa, C("diag_swa", 0, BUCKETS + 1), True, True, ()),
                           (b2.ap[0:MOBA_H, 0:TOEP], relb[:, SWA_H:BIAS_H], C("diag_moba", 0, BUCKETS + 1), True, True, ())],
                          after=[relb_loaded, const_loaded, b.free, b2.free])
        diag_sem = sem("diag_stored")
        d1 = evac(diag_sb[0:SWA_H, :], b.ap[0:SWA_H, 0:TOEP], done, dve)
        d1 = pool.load(diag_sem, [(diag_dram[0:SWA_H, :], diag_sb[0:SWA_H, :])], after=d1)
        d2 = evac(diag_sb[0:MOBA_H, :], b2.ap[0:MOBA_H, 0:TOEP], [done, d1], dve)
        d2 = pool.load(diag_sem, [(diag_dram[SWA_H:BIAS_H, :], diag_sb[0:MOBA_H, :])], after=d2)
        banks.release(b, d1)
        banks.release(b2, d2)
        toep_pool = Pool([Buffer(toep_a[:, i * S:(i + 1) * S], sem(f"toep{i}_loaded")) for i in range(8)])

        def toeplitz(head):
            t = toep_pool.take()
            src = bass.AP(diag_dram.tensor, head * TOEP, [[1, P], [1, S]])
            t.token = pool.load(t.landed, [(t.ap, src)], after=[d2, x_ready, t.free])
            return t

        def forget_gate():
            b = banks.take()
            z = small(2 * S, FOX_H)
            zz, ez = z[:, 0:S], z[:, S:2 * S]
            done = pe.matmuls([(b.ap[0:FOX_H, 0:S], wfc[:, k, :], h[:, k, :], k == 0, k == KT - 1, h_ready[k])
                               for k in range(KT)], after=[wfc_loaded, b.free])
            r = ts(zz, b.ap[0:FOX_H, 0:S], bfg[:, 0:1], ALU.add, after=[done, bfg_loaded])
            banks.release(b, r)
            r = stt(ez, zz, -1.0, zz, ALU.mult, ALU.max, r)
            r = af(ez, ez, ACT.Exp, r, scale=-1.0)
            r = af(ez, ez, ACT.Ln, r, bias=1.0)
            r = stt(ez, zz, 0.0, ez, ALU.min, ALU.subtract, r)
            one = dve(lambda e: e.memset(fox_l[0:2, :], 1.0), cut_at)
            one2 = dve(lambda e: e.memset(fox_rt[0:2, :], 1.0), cut_at)
            r = dve(lambda e: e.tensor_tensor_scan(zz, ones[0:FOX_H, 0:1].broadcast_to([FOX_H, S]), ez, 0.0,
                                                   ALU.mult, ALU.add), r)
            r2 = ts(ez, zz, -1.0, ALU.mult, after=r)
            s = sem("fox_rows")
            head = lambda rows, n: rows[:, n * S:(n + 1) * S]
            return pool.load(s, [(head(fox_l[0:1, :], n), zz[n:n + 1, :]) for n in range(FOX_H)] +
                             [(head(fox_rt[1:2, :], n), ez[n:n + 1, :]) for n in range(FOX_H)], after=[r, r2, one, one2])

        def keep(dst, on, scale=None, also=None):
            def take(src, done):
                if scale is not None:
                    r = af(dst, src, ACT.Copy, [done, cut_at], scale=scale) if on is act else \
                        ts(dst, src, scale, ALU.mult, after=[done, cut_at])
                else:
                    r = evac(dst, src, [done, cut_at], on)
                if also is not None:
                    also.append(r)
                return r
            return take

        made = {n: [] for n in ("qa", "ka", "va", "qc", "kc", "vc", "qd", "kd", "vd", "pad", "up", "uq", "uk", "uv")}

        def heads_qkv():
            for i in range(2):
                u = unit([(lambda s, g=g, y=y: s.rearrange("p (k y g x) -> p k y g x", k=KT, y=2, g=KV_H)[:, :, y, g, :],
                           w_in[:, (4 * g + 2 * i + y) * HD:(4 * g + 2 * i + y + 1) * HD]
                           .rearrange("(k p) x -> p k x", p=P)) for g in range(KV_H) for y in range(2)])
                project(u, h, h_ready, keep(qa[:, 2 * i:2 * i + 2, :], act, HD ** -0.5, made["qa"]))
                yield
            u = columns(w_in, OFF["ka"])
            w = u.ap[:, :].rearrange("p (k n) -> p k n", k=KT)
            b = banks.take()
            done = pe.matmuls([(b.ap[:, 0:S], w[:, k, 0:P], h[:, k, :], k == 0, k == KT - 1, h_ready[k])
                               for k in range(KT)] +
                              [(b.ap[:, S + t * P:S + (t + 1) * P], h[:, k, t * P:(t + 1) * P], w[:, k, P:2 * P],
                                k == 0, k == KT - 1, ()) for t in range(TT) for k in range(KT)],
                              after=[b.free, u.token])
            ring.release(u, done)
            made["ka"].append(evac(ka, b.ap[:, 0:S], [done, cut_at], dve))
            made["va"].append(evac(va, b.ap[:, S:2 * S].rearrange("p (t n) -> p t n", t=TT),
                                   [done, cut_at, made["ka"]], act))
            banks.release(b, [made["ka"], made["va"]])
            yield
            for q, k, v, qt, kt_, vt in (("qd", "kd", "vd", qd, kd, vd), ("qc", "kc", "vc", qc, kc, vc)):
                for i in range(2):
                    project(columns(w_in, OFF[q] + i * 256), h, h_ready,
                            keep(qt[:, 2 * i:2 * i + 2, :], act, HD ** -0.5, made[q]))
                    project(columns(w_in, OFF[k] + i * 256), h, h_ready,
                            keep(kt_[:, 2 * i:2 * i + 2, :], dve, None, made[k]))
                    project_tokens(columns(w_in, OFF[v] + i * 256), h, h_ready,
                                   keep(vt[:, :, i * 256:(i + 1) * 256], act, None, made[v]))
                    yield

        PARTS = (slice(0, 256), slice(256, 384))

        def softmax(bank, done, stat, sink=None):
            e = score_pool.take()
            nm, sm = stat.ap[:, 0:2], stat.ap[:, 2:4]
            for i, c in enumerate(PARTS):
                top = neg_max(nm[:, i:i + 1], bank.ap[:, c], [done, stat.free])
            if sink is not None:
                top = ts(nm, nm, neg_sinks[:, sink:sink + 1], ALU.min, after=[top, neg_ready])
            for i, c in enumerate(PARTS):
                ex = af(e.ap[:, c], bank.ap[:, c], ACT.Exp, [top, e.free, cut_at], bias=nm[:, i:i + 1],
                        accum_out=sm[:, i:i + 1])
            banks.release(bank, [top, ex])
            if sink is not None:
                es = stat.ap[:, 4:6]
                ex2 = af(es, nm, ACT.Exp, top, bias=sinks[:, sink:sink + 1])
                ex = tt(sm, sm, es, ALU.add, [ex, ex2])
            r = recip(sm, sm, ex)
            return e, r, sm

        stats = Pool([Buffer(small(6)) for _ in range(6)])

        neg_sinks = small(SWA_H)
        neg_ready = ts(neg_sinks, sinks, -1.0, ALU.mult, after=sinks_loaded)

        def attend(e, ready, values, out_ap, out_free):
            b = banks.take()
            done = pe.transposes([(b.ap[:, 0:128], e.ap[:, 256:384]), (b.ap[:, 128:256], e.ap[:, 0:128]),
                                  (b.ap[:, 256:384], e.ap[:, 128:256])], ident, after=[ready, b.free])
            score_pool.release(e, done)
            p = prob_pool.take()
            got = evac(p.ap, b.ap[:, 0:384], [done, p.free, cut_at], act)
            banks.release(b, got)
            yield
            done = pe.matmuls([(out_ap, values(0), p.ap[:, 0:256], True, False, ()),
                               (out_ap[:, 128:256], values(1), p.ap[:, 256:384], False, True, ())],
                              after=[got, out_free])
            prob_pool.release(p, done)
            yield done

        def normalize(e, r, sm):
            for i, c in enumerate(PARTS):
                r = ts(e.ap[:, c], e.ap[:, c], sm[:, i:i + 1], ALU.mult, after=r)
            return r

        def head_scores(bank, q, k, extra, after):
            prods = []
            for c, qs, ks, hs in ((PARTS[0], slice(128, 256), slice(0, 256), slice(0, 256)),
                                  (PARTS[1], slice(0, 128), slice(0, 128), slice(128, 256))):
                prods.append((bank.ap[:, c], q[:, qs], k[:, ks], True, False, ()))
                for n, (l, r) in enumerate(extra(qs, ks, hs)):
                    prods.append((bank.ap[:, c], l, r, False, n == len(extra(qs, ks, hs)) - 1, ()))
            return pe.matmuls(prods, after=[bank.free, after])

        def attention(kind):
            for pair in range(4):
                out_b = banks.take()
                dones = []
                for j in range(2):
                    stat = stats.take()
                    bank = banks.take()
                    rows = slice(j * HD, (j + 1) * HD)
                    if kind == "swa":
                        head = pair + 4 * j
                        t = toeplitz(head)
                        done = head_scores(bank, qa[rows, pair, :], ka[rows, :],
                                           lambda qs, ks, hs: [(C("flip"), t.ap[:, hs])],
                                           [made["qa"], made["ka"], t.token])
                        toep_pool.release(t, done)
                        e, r, sm = softmax(bank, done, stat, sink=head)
                        vals, dep = (lambda kb, j=j: va[:, kb, j * HD:(j + 1) * HD]), made["va"]
                    elif kind == "moba":
                        head = 2 * pair + j
                        t = toeplitz(SWA_H + head)
                        done = head_scores(bank, qd[rows, pair, :], kd[rows, pair, :],
                                           lambda qs, ks, hs: [(C("flip"), t.ap[:, hs])],
                                           [made["qd"], made["kd"], t.token])
                        toep_pool.release(t, done)
                        e, r, sm = softmax(bank, done, stat)
                        vals, dep = (lambda kb, head=head: vd[:, kb, head * HD:(head + 1) * HD]), made["vd"]
                    else:
                        head = 2 * pair + j
                        fl = fox_l[0:2, head * S:(head + 1) * S]
                        fr = fox_rt[0:2, head * S:(head + 1) * S]
                        done = head_scores(bank, qc[rows, pair, :], kc[rows, pair, :],
                                           lambda qs, ks, hs: [(fl[:, qs], fr[:, ks]), (ident, C("causal")[:, hs])],
                                           [made["qc"], made["kc"], fox_ready])
                        e, r, sm = softmax(bank, done, stat)
                        vals, dep = (lambda kb, head=head: vc[:, kb, head * HD:(head + 1) * HD]), made["vc"]
                    r = normalize(e, r, sm)
                    stats.release(stat, r)
                    yield
                    for step in attend(e, [r, dep], vals, out_b.ap[rows, 0:S], out_b.free):
                        if step is None:
                            yield
                        else:
                            dones.append(step)
                    yield
                tile = {"swa": 0, "fox": 8, "moba": 12}[kind] + pair
                got = evac(yt[:, tile, :], out_b.ap[:, 0:S], [dones, cut_at], dve)
                y_ready[tile] = got
                banks.release(out_b, got)

        y_ready = [()] * 16

        PAD = CONV_W - 1
        glu = area(BT * (PAD + S)).rearrange("p (n s) -> p n s", n=BT)
        conv = tiles(area(BT * S), BT)
        tanh_pool = Pool([Buffer(area(S)) for _ in range(2)])

        def conv_input():
            zero = dve(lambda e: e.memset(glu[:, :, 0:PAD], 0.0), cut_at)
            for c in range(BT):
                u = unit([(lambda s, j=j: s[:, :].rearrange("p (k n) -> p k n", k=KT)[:, :, j * P:(j + 1) * P],
                           w_in[:, OFF["ub"] + j * BR + c * P:OFF["ub"] + j * BR + (c + 1) * P]
                           .rearrange("(k p) n -> p k n", p=P)) for j in range(2)])

                def take(src, done):
                    t = tanh_pool.take()
                    r = af(t.ap, src[:, 1, :], ACT.Tanh, [done, t.free, cut_at], scale=0.5)
                    r = stt(glu[:, c, PAD:PAD + S], t.ap, 1.0, src[:, 0, :], ALU.add, ALU.mult, [r, zero])
                    tanh_pool.release(t, r)
                    made["pad"].append(r)
                    return r
                project(u, h, h_ready, take)
                yield

        def conv_taps():
            last = [[] for _ in range(BT)]
            for j in range(CONV_W):
                for c in range(BT):
                    w = cols_sb[:, cw0 + j * BT + c:cw0 + j * BT + c + 1]
                    if j == 0:
                        last[c] = ts(conv[:, c, :], glu[:, c, 0:S], w, ALU.mult, col("conv_b", c), ALU.add,
                                     after=[made["pad"], taps_ready, cut_at])
                    else:
                        last[c] = stt(conv[:, c, :], glu[:, c, j:j + S], w, conv[:, c, :], ALU.mult, ALU.add, last[c])
                if j % 2:
                    yield
            b = banks.take()
            done = pe.matmuls([(b.ap[:, 0:S], ones, conv[:, c, :], c == 0, c == BT - 1, last[c]) for c in range(BT)],
                              after=b.free)
            mean = rstd_sb[:, S:2 * S]
            r = ts(mean, b.ap[:, 0:S], 1.0 / BR, ALU.mult, after=done)
            banks.release(b, r)
            r = tt(conv, conv, mean.rearrange("p (o s) -> p o s", o=1).broadcast_to([P, BT, S]), ALU.subtract, r)
            sq = glu[:, :, 0:S]
            r2 = af(sq, conv, ACT.Square, r)
            b = banks.take()
            done = pe.matmuls([(b.ap[:, 0:S], ones, sq[:, c, :], c == 0, c == BT - 1, r2) for c in range(BT)],
                              after=b.free)
            yield
            root = inverse_root(b.ap[:, 0:S], BR, EPS1, done, mean)
            banks.release(b, root)
            r = tt(conv, conv, mean.rearrange("p (o s) -> p o s", o=1).broadcast_to([P, BT, S]), ALU.mult, root)
            for c in range(BT):
                r1 = ts(conv[:, c, :], conv[:, c, :], col("conv_ln_g", c), ALU.mult, col("conv_ln_b", c), ALU.add,
                        after=[r, cols_ready])
                r2 = af(sq[:, c, :], conv[:, c, :], ACT.Tanh, [r1, done], scale=0.5)
                r3 = ts(conv[:, c, :], conv[:, c, :], 0.5, ALU.mult, after=[r1, r2])
                y_ready[4 + c] = stt(yt[:, 4 + c, :], sq[:, c, :], 1.0, conv[:, c, :], ALU.add, ALU.mult,
                                     [r2, r3, cut_at])

        gate_ready = [()] * 32
        half_b = small(32)
        half_ready = ts(half_b, cols_sb[:, col_at["b_gate"]:col_at["b_gate"] + 32], 0.5, ALU.mult, after=cols_ready)

        def gates():
            for i in range(16):
                def take(src, done):
                    for j in range(2):
                        r = af(gate[:, 2 * i + j, :], src[:, j, :], ACT.Tanh, [done, half_ready, cut_at],
                               bias=half_b[:, 2 * i + j:2 * i + j + 1], scale=0.5)
                        gate_ready[2 * i + j] = r
                    return r
                project(columns(w_in, OFF["gz"] + i * 256), h, h_ready, take)
                yield

        fox_ready = forget_gate()
        interleave(conv_input())
        interleave(heads_qkv(), conv_taps())
        interleave(attention("swa"), attention("moba"), attention("fox"), gates())

        free_at[0] = qkv0
        att_end = fence()
        merged = tiles(area(KT * S), KT)
        prod_pool = Pool([Buffer(area(2 * S)) for _ in range(2)])
        m_ready = [()] * KT
        for n in (1, 0, 3, 2):
            for half in range(2):
                w_br = a["w_br"][0, n]
                cs = slice(half * 512, (half + 1) * 512)
                if n == 0:
                    wv = w_br[:, cs].rearrange("(g h d) n -> g d h n", g=KV_H, h=4)
                    u = unit([(lambda s, g=g: s[g * HD:(g + 1) * HD, :].rearrange("p (k n) -> p k n", k=BT), wv[g])
                              for g in range(KV_H)])
                else:
                    u = unit([(lambda s: s[:, :].rearrange("p (k n) -> p k n", k=BT),
                               w_br[:, cs].rearrange("(k p) n -> p k n", p=P))])
                w = u.ap[:, :].rearrange("p (k n) -> p k n", k=BT)
                for jj in range(2):
                    b = banks.take()
                    done = pe.matmuls([(b.ap[:, j * S:(j + 1) * S], w[:, k, (2 * jj + j) * P:(2 * jj + j + 1) * P],
                                        yt[:, 4 * n + k, :], k == 0, k == BT - 1, y_ready[4 * n + k])
                                       for j in range(2) for k in range(BT)], after=[b.free, u.token])
                    d0 = half * 4 + 2 * jj
                    g = gate[:, n * KT + d0:n * KT + d0 + 2, :]
                    src = b.ap[:, :].rearrange("p (n s) -> p n s", n=2)
                    dep = [done, gate_ready[n * KT + d0], gate_ready[n * KT + d0 + 1], att_end]
                    if n == 1:
                        r = stt(merged[:, d0:d0 + 2, :], g, 1.0, src, ALU.add, ALU.mult, dep)
                        banks.release(b, r)
                    else:
                        t = prod_pool.take()
                        tv = t.ap.rearrange("p (n s) -> p n s", n=2)
                        r = stt(tv, g, 1.0, src, ALU.add, ALU.mult, [dep, t.free])
                        banks.release(b, r)
                        r = tt(merged[:, d0:d0 + 2, :], merged[:, d0:d0 + 2, :], tv, ALU.add, [r, m_ready[d0]])
                        prod_pool.release(t, r)
                    m_ready[d0] = m_ready[d0 + 1] = r
                ring.release(u, done)

        def add_residual(w, src, ready, n_tiles_in, scale=None):
            got = []
            for i in range(4):
                def take(ps, done):
                    xs = x[:, 2 * i:2 * i + 2, :]
                    if scale is None:
                        r = tt(xs, ps, xs, ALU.add, done)
                    else:
                        r = stt(xs, ps, scale, xs, ALU.mult, ALU.add, done)
                    got.extend([r, r])
                    return r
                project(columns(w, i * 256), src, ready, take)
            return got

        x_ready = add_residual(a["w_out"][0], merged, m_ready, KT, scale=0.5)

        h_ready = rms(x, x_ready, "ln2_g", EPS1, h, fence())
        free_at[0] = qkv0
        ff_start = fence()
        uf_pool = Pool([Buffer(area(2 * S)) for _ in range(3)])
        th_pool = Pool([Buffer(area(S)) for _ in range(2)])
        ff = tiles(gate_a[:, 0:FT * S], FT)
        ff_ready = [()] * FT
        w_up = a["w_up"][0]
        for i in range(FT):
            u = unit([(lambda s, j=j: s[:, :].rearrange("p (k n) -> p k n", k=KT)[:, :, j * P:(j + 1) * P],
                       w_up[:, j * D_FF + i * P:j * D_FF + (i + 1) * P].rearrange("(k p) n -> p k n", p=P))
                      for j in range(2)])

            def take(src, done):
                t = uf_pool.take()
                tv = t.ap.rearrange("p (n s) -> p n s", n=2)
                for j in range(2):
                    f = j * FT + i
                    r0 = af(tv[:, j, :], src[:, j, :], ACT.Identity, [done, t.free, ff_start, cols_ready],
                            bias=col("ffn_b", f), scale=col("tap2", f))
                for j in range(2):
                    f = j * FT + i
                    r = r0
                    for lag, tap in ((1, "tap1"), (2, "tap0")):
                        r = stt(tv[:, j, lag:S], src[:, j, 0:S - lag], col(tap, f), tv[:, j, lag:S], ALU.mult, ALU.add, r)
                    if j == 0:
                        q = th_pool.take()
                        r1 = af(q.ap, tv[:, 0, :], ACT.Tanh, [r, q.free, ff_start], scale=0.5)
                        r1 = stt(q.ap, q.ap, 1.0, tv[:, 0, :], ALU.add, ALU.mult, r1)
                ff_ready[i] = tt(ff[:, i, :], q.ap, tv[:, 1, :], ALU.mult, [r, r1])
                th_pool.release(q, ff_ready[i])
                uf_pool.release(t, ff_ready[i])
                return r
            project(u, h, h_ready, take)

        acc = [banks.take() for _ in range(4)]
        w_down = a["w_down"][0]
        for i in range(FT // 2):
            u = unit([(lambda s: s[:, :].rearrange("p (k n) -> p k n", k=2),
                       w_down[i * 256:(i + 1) * 256, :].rearrange("(k p) n -> p k n", p=P))])
            w = u.ap[:, :].rearrange("p (k n) -> p k n", k=2)
            prods = []
            for kk in range(2):
                f = 2 * i + kk
                for d in range(KT):
                    prods.append((acc[d // 2].ap[:, (d % 2) * S:(d % 2 + 1) * S], w[:, kk, d * P:(d + 1) * P],
                                  ff[:, f, :], f == 0 and d % 2 == 0, f == FT - 1, ff_ready[f]))
            done = pe.matmuls(prods, after=[u.token, [b.free for b in acc]])
            ring.release(u, done)
        x_ready = []
        for j in range(4):
            r = stt(x[:, 2 * j:2 * j + 2, :], acc[j].ap[:, :].rearrange("p (n s) -> p n s", n=2), 0.5,
                    x[:, 2 * j:2 * j + 2, :], ALU.mult, ALU.add, done)
            banks.release(acc[j], r)
            x_ready += [r, r]

        h_ready = rms(x, x_ready, "final_g", EPS1, h, fence())
        x_ready = []
        for j in range(4):
            r = evac(x[:, 2 * j:2 * j + 2, :], h[:, 2 * j:2 * j + 2, :], h_ready, act if j % 2 else dve)
            x_ready += [r, r]

        block2 = fence()
        free_at[0] = 0
        up, uq, uk = (tiles(area(BT * S), BT) for _ in range(3))
        uv = area(TT * BR).rearrange("p (t n) -> p t n", t=TT)
        mix = tiles(area(KT * S), KT)
        sine, cosine, turns = (area(S) for _ in range(3))
        posf = area(S)
        score_pool = Pool([Buffer(area(384)) for _ in range(4)])
        prob_pool = Pool([Buffer(area(384)) for _ in range(3)])
        memt = tiles(area(KT * S), KT)
        memx = area(TT * D).rearrange("p (t d) -> p t d", t=TT)
        ck = tiles(area(KT * S), KT)
        cv = area(TT * D).rearrange("p (t d) -> p t d", t=TT)
        cut_at = block2
        mem_loaded = small_load("mem_loaded", memx, a["mem_2"][0].rearrange("(t p) d -> p t d", p=P), queue=pool,
                                after=block2)

        lamv = small(4)
        lprod = small(HD)
        for i in range(2):
            r = tt(lprod, lams[:, 2 * i * HD:(2 * i + 1) * HD], lams[:, (2 * i + 1) * HD:(2 * i + 2) * HD], ALU.mult,
                   [lam_loaded, r if i else ()])
            r = dve(lambda e, i=i: e.tensor_reduce(lamv[:, i:i + 1], lprod, AX.X, ALU.add), r)
        r = af(lamv[:, 0:2], lamv[:, 0:2], ACT.Exp, r)
        r = tt(lamv[:, 2:3], lamv[:, 0:1], lamv[:, 1:2], ALU.subtract, r)
        lam_ready = ts(lamv[:, 2:3], lamv[:, 2:3], LAM_INIT, ALU.add, after=r)

        r = dve(lambda e: e.tensor_copy(posf, pos_i[:, :]), [pos_loaded, block2])
        r = ts(posf, posf, C("freq"), ALU.mult, after=r)
        magic = 1.5 * 2 ** 23
        r = ts(turns, posf, 1.0 / (2 * math.pi), ALU.mult, magic, ALU.add, after=r)
        r = ts(turns, turns, magic, ALU.subtract, after=r)
        c1 = 6.28125
        c2 = float(np.float32(np.round((2 * math.pi - c1) * 2 ** 20) / 2 ** 20))
        c3 = 2 * math.pi - c1 - c2
        for c in (c1, c2, c3):
            r = stt(posf, turns, -c, posf, ALU.mult, ALU.add, r)
        rs = af(sine, posf, ACT.Sin, r)
        rc = af(cosine, posf, ACT.Sin, r, scale=0.5)
        rc = tt(cosine, cosine, cosine, ALU.mult, rc)
        rot_ready = [rs, ts(cosine, cosine, -2.0, ALU.mult, 1.0, ALU.add, after=rc)]

        h_ready = rms(x, x_ready, "attn_g", EPS2, h, fence())
        w_in2 = a["w_in_2"][0]

        def rotate(dst, i, ready):
            b = banks.take()
            done = pe.matmuls([(b.ap[:, 0:S], C("rot"), dst[:, i, :], True, True, ready)], after=b.free)
            r1 = tt(dst[:, i, :], dst[:, i, :], cosine, ALU.mult, [done, rot_ready])
            t = rot_tmp.take()
            r2 = tt(t.ap, b.ap[:, 0:S], sine, ALU.mult, [done, rot_ready, t.free])
            banks.release(b, r2)
            r = tt(dst[:, i, :], dst[:, i, :], t.ap, ALU.add, [r1, r2])
            rot_tmp.release(t, r)
            return r

        rot_tmp = Pool([Buffer(area(S)) for _ in range(2)])
        rotated = {"uq": [()] * BT, "uk": [()] * BT}
        for i in range(2):
            project(columns(w_in2, BR + i * 256), h, h_ready,
                    keep(uq[:, 2 * i:2 * i + 2, :], act, HD ** -0.5, made["uq"]))
            project(columns(w_in2, 2 * BR + i * 256), h, h_ready,
                    keep(uk[:, 2 * i:2 * i + 2, :], dve, None, made["uk"]))
            for j in range(2 * i, 2 * i + 2):
                rotated["uq"][j] = rotate(uq, j, made["uq"][i])
                rotated["uk"][j] = rotate(uk, j, made["uk"][i])
        for i in range(2):
            project_tokens(columns(w_in2, 3 * BR + i * 256), h, h_ready,
                           keep(uv[:, :, i * 256:(i + 1) * 256], act, None, made["uv"]))
        for i in range(2):
            project(columns(w_in2, i * 256), h, h_ready, keep(up[:, 2 * i:2 * i + 2, :], act, None, made["up"]))

        mix_ready = [()] * KT

        def pooling():
            M = 16
            two = [area(M + S) for _ in range(2)]
            wp = unit([(lambda s: s[:, 0:BT * P].rearrange("p (g n) -> p g n", g=BT),
                        a["w_pool_2"][0].rearrange("g p n -> p g n"))])
            wpv = wp.ap[:, 0:BT * P].rearrange("p (g n) -> p g n", g=BT)
            zero = [dve(lambda e, t=t: e.memset(t[:, 0:M], 0.0), block2) for t in two]
            b = None
            r = ()
            for g, win in enumerate(POOL_W):
                u = up[:, g, :]
                r = dve(lambda e, u=u: e.tensor_copy(two[0][:, M:M + S], u), [made["up"], zero, r])
                cur = 0
                for i in range(g + 1):
                    s, d = two[cur], two[1 - cur]
                    r = tt(d[:, M:M + S], s[:, M:M + S], s[:, M - 2 ** i:M - 2 ** i + S], ALU.add, r)
                    cur = 1 - cur
                s, d = two[cur], two[1 - cur]
                r = stt(d[:, M:M + S], s[:, M:M + S], 1.0 / win, u, ALU.mult, ALU.subtract, r)
                r = tt(d[:, M:2 * M], s[:, M:2 * M], C("invc")[:, g * M:(g + 1) * M], ALU.mult, r)
                r = tt(d[:, M:2 * M], d[:, M:2 * M], u[:, 0:M], ALU.subtract, r)
                b = banks.take()
                done = pe.matmuls([(b.ap[:, 0:S], wpv[:, g, :], d[:, M:M + S], True, True, ())],
                                  after=[r, b.free, wp.token])
                mix_ready[g] = r = ts(mix[:, g, :], b.ap[:, 0:S], col("pool_scale", g), ALU.mult, after=[done, block2])
                banks.release(b, r)
                yield
            ring.release(wp, done)

        def diff():
            for head in range(DIFF_H):
                maps = []
                for m in range(2):
                    stat, bank = stats.take(), banks.take()
                    rows = slice(m * HD, (m + 1) * HD)
                    done = head_scores(bank, uq[rows, head, :], uk[rows, head, :],
                                       lambda qs, ks, hs: [(ident, C("chunk1")[:, hs])],
                                       [rotated["uq"][head], rotated["uk"][head]])
                    e, r, sm = softmax(bank, done, stat)
                    maps.append((e, r, sm, stat))
                (e0, r0, s0, st0), (e1, r1, s1, st1) = maps
                r = ts(s1, s1, lamv[:, 2:3], ALU.mult, after=[r1, lam_ready])
                for i, c in enumerate(PARTS):
                    r = ts(e1.ap[:, c], e1.ap[:, c], s1[:, i:i + 1], ALU.mult, after=r)
                    r = stt(e0.ap[:, c], e0.ap[:, c], s0[:, i:i + 1], e1.ap[:, c], ALU.mult, ALU.subtract, [r, r0])
                stats.release(st0, r)
                stats.release(st1, r)
                score_pool.release(e1, r)
                yield
                ob = banks.take()
                for step in attend(e0, [r, made["uv"]], lambda kb: uv[:, kb, head * P:(head + 1) * P],
                                   ob.ap[:, 0:S], ob.free):
                    if step is None:
                        yield
                    else:
                        done = step
                o = mix[:, BT + head, :]
                r = evac(o, ob.ap[:, 0:S], [done, block2], dve)
                banks.release(ob, r)
                t = rot_tmp.take()
                r2 = af(t.ap, o, ACT.Square, [r, t.free])
                b = banks.take()
                done = pe.matmuls([(b.ap[:, 0:S], ones, t.ap, True, True, ())], after=[r2, b.free])
                root = inverse_root(b.ap[:, 0:S], DIFF_V, EPS2, [done], t.ap)
                banks.release(b, root)
                r = stt(o, o, col("subln"), t.ap, ALU.mult, ALU.mult, root)
                mix_ready[BT + head] = r = ts(o, o, 1.0 - LAM_INIT, ALU.mult, after=r)
                rot_tmp.release(t, r)
                yield

        def memory_side():
            nonlocal ck_ready, cv_ready
            m_r = turn(memt, memx, [mem_loaded, block2])
            yield
            mr = rms(memt, m_r, "mem_g", EPS2, memn, block2)
            yield
            w = a["w_ckv_2"][0]
            for i in range(4):
                project(columns(w, i * 256), memn, mr, keep(ck[:, 2 * i:2 * i + 2, :], act, None, ck_ready))
                yield
            for i in range(4):
                project_tokens(columns(w, D + i * 256), memn, mr,
                               keep(cv[:, :, i * 256:(i + 1) * 256], dve, None, cv_ready))
                yield

        memn = tiles(area(KT * S), KT)
        ck_ready, cv_ready = [], []
        interleave(diff(), memory_side(), pooling())
        x_ready = add_residual(a["w_out_2"][0], mix, mix_ready, KT)

        h_ready = rms(x, x_ready, "xattn_g", EPS2, h, fence())
        cq, co = memt, mix
        cq_ready, co_ready = [], [()] * KT
        before = fence()
        cut_at = before
        for i in range(4):
            project(columns(a["w_cq_2"][0], i * 256), h, h_ready,
                    keep(cq[:, 2 * i:2 * i + 2, :], act, X_HD ** -0.5, cq_ready))
        wide = [Buffer(memx.rearrange("p t d -> p (t d)")[:, i * 512:(i + 1) * 512]) for i in range(4)]
        es, ps = Pool(wide[0:2]), Pool(wide[2:4])

        def cross():
            for head in range(X_H):
                stat, bank, e = stats.take(), banks.take(), es.take()
                prods = []
                for t in range(TT):
                    for d in range(2):
                        f = 2 * head + d
                        prods.append((bank.ap[:, t * S:(t + 1) * S], cq[:, f, t * P:(t + 1) * P], ck[:, f, :],
                                      d == 0, d == 1, ()))
                done = pe.matmuls(prods, after=[bank.free, cq_ready, ck_ready])
                nm, sm = stat.ap[:, 0:2], stat.ap[:, 2:4]
                r = neg_max(nm, bank.ap[:, :].rearrange("p (t s) -> p t s", t=TT), [done, stat.free])
                for t in range(TT):
                    ex = af(e.ap[:, t * S:(t + 1) * S], bank.ap[:, t * S:(t + 1) * S], ACT.Exp, [r, e.free, before],
                            bias=nm[:, t:t + 1], accum_out=sm[:, t:t + 1])
                banks.release(bank, [r, ex])
                r = recip(sm, sm, ex)
                for t in range(TT):
                    r = ts(e.ap[:, t * S:(t + 1) * S], e.ap[:, t * S:(t + 1) * S], sm[:, t:t + 1], ALU.mult, after=r)
                stats.release(stat, r)
                yield
                b = banks.take()
                done = pe.transposes([(b.ap[:, kb * S + t * P:kb * S + (t + 1) * P],
                                       e.ap[:, t * S + kb * P:t * S + (kb + 1) * P])
                                      for kb in range(2) for t in range(TT)], ident, after=[r, b.free])
                es.release(e, done)
                p = ps.take()
                got = evac(p.ap, b.ap[:, :], [done, p.free, before], act)
                banks.release(b, got)
                yield
                ob = banks.take()
                done = pe.matmuls([(ob.ap[:, d * S:(d + 1) * S], cv[:, kb, head * X_HD + d * P:head * X_HD + (d + 1) * P],
                                    p.ap[:, kb * S:(kb + 1) * S], kb == 0, kb == 1, ())
                                   for d in range(2) for kb in range(2)], after=[got, ob.free, cv_ready])
                ps.release(p, done)
                r = evac(co[:, 2 * head:2 * head + 2, :], ob.ap[:, :].rearrange("p (n s) -> p n s", n=2), [done, before], dve)
                banks.release(ob, r)
                co_ready[2 * head] = co_ready[2 * head + 1] = r
                yield

        interleave(cross())
        x_ready = add_residual(a["w_co_2"][0], co, co_ready, KT)

        h_ready = rms(x, x_ready, "ffn_g", EPS2, h, fence())

        moe0 = fence()
        free_at[0] = 0
        b = banks.take()
        done = pe.matmuls([(b.ap[:, t * NE:(t + 1) * NE], h[:, k, t * P:(t + 1) * P], wrt[:, k, :],
                            k == 0, k == KT - 1, h_ready[k]) for t in range(TT) for k in range(KT)],
                          after=[b.free, wrt_loaded])

        def expert_table(n=NE):
            return area(TT * n).rearrange("p (t n) -> p t n", t=TT)

        logit, mask, tmp, tmp2, gates_x, pos_x = (expert_table() for _ in range(6))
        top8 = area(TT * 8).rearrange("p (t n) -> p t n", t=TT)
        cnt, ovf = area(NE), area(NE)
        scal = area(16)
        r = tt(logit, b.ap[:, 0:TT * NE].rearrange("p (t n) -> p t n", t=TT),
               brt.rearrange("p (o n) -> p o n", o=1).broadcast_to([P, TT, NE]), ALU.add, [done, brt_loaded, moe0])
        banks.release(b, r)
        for t in range(TT):
            r = dve(lambda e, t=t: e.max(top8[:, t, :], logit[:, t, :]), r)
            least = top8[:, t, TOPK - 1:TOPK]
            r = dve(lambda e, t=t, least=least: e.tensor_scalar(mask[:, t, :], logit[:, t, :], least, 0.0, ALU.is_gt,
                                                                ALU.add, accum_out=scal[:, t:t + 1]), r)
            r = ts(scal[:, t:t + 1], scal[:, t:t + 1], -1.0, ALU.mult, float(TOPK), ALU.add, after=r)
            r = ts(tmp[:, t, :], logit[:, t, :], least, ALU.is_equal, after=r)
            r = dve(lambda e, t=t: e.tensor_tensor_scan(tmp2[:, t, :], ones[:, 0:NE], tmp[:, t, :], 0.0, ALU.mult,
                                                        ALU.add), r)
            r = stt(tmp[:, t, :], tmp2[:, t, :], scal[:, t:t + 1], tmp[:, t, :], ALU.is_le, ALU.mult, r)
            r = tt(mask[:, t, :], mask[:, t, :], tmp[:, t, :], ALU.add, r)
            mask_ready = r
            r = ts(scal[:, 2 + t:3 + t], top8[:, t, 0:1], -1.0, ALU.mult, after=r)
            ex = af(gates_x[:, t, :], logit[:, t, :], ACT.Exp, r, bias=scal[:, 2 + t:3 + t])
            r = tt(gates_x[:, t, :], gates_x[:, t, :], mask[:, t, :], ALU.mult, ex)
            r = dve(lambda e, t=t: e.tensor_reduce(scal[:, 4 + t:5 + t], gates_x[:, t, :], AX.X, ALU.add), r)
            r = recip(scal[:, 4 + t:5 + t], scal[:, 4 + t:5 + t], r)
            r = ts(gates_x[:, t, :], gates_x[:, t, :], scal[:, 4 + t:5 + t], ALU.mult, after=r)
        gates_ready = r

        b = banks.take()
        done = pe.matmuls([(b.ap[:, 0:NE], C("tri"), mask[:, 0, :], True, True, ()),
                           (b.ap[:, NE:2 * NE], C("tri"), mask[:, 1, :], True, False, ()),
                           (b.ap[:, NE:2 * NE], ones, mask[:, 0, :], False, True, ()),
                           (b.ap[:, 2 * NE:3 * NE], ones, mask[:, 0, :], True, False, ()),
                           (b.ap[:, 2 * NE:3 * NE], ones, mask[:, 1, :], False, True, ())],
                          after=[mask_ready, b.free])
        r = stt(pos_x, b.ap[:, 0:TT * NE].rearrange("p (t n) -> p t n", t=TT), 1.0, mask, ALU.add, ALU.mult, done)
        pos_ready = ts(pos_x, pos_x, -1.0, ALU.add, after=r)
        r = evac(cnt, b.ap[:, 2 * NE:3 * NE], done, dve)
        banks.release(b, [r, pos_ready])
        cnt_ready = r
        r = dve(lambda e: e.tensor_reduce(scal[:, 6:7], cnt, AX.X, ALU.max), r)
        flag_ready = ts(flag_sb[:, 0:1], scal[:, 6:7], -float(CAP), ALU.add, 0.0, ALU.max, after=r)

        h_tok = area(TT * D).rearrange("p (t d) -> p t d", t=TT)
        x_tok = area(TT * D).rearrange("p (t d) -> p t d", t=TT)

        def turn_back(dst, src, ready):
            got = []
            for t in range(TT):
                for q in range(2):
                    b = banks.take()
                    done = pe.transposes([(b.ap[:, j * P:(j + 1) * P], src[:, 4 * q + j, t * P:(t + 1) * P])
                                          for j in range(4)], ident, after=[ready, b.free])
                    got.append(evac(dst[:, t, q * 512:(q + 1) * 512], b.ap[:, :], [done, moe0], act if q else dve))
                    banks.release(b, got[-1])
            return got
        htok_ready = turn_back(h_tok, h, h_ready)
        xtok_ready = turn_back(x_tok, x, x_ready)

        gates_e = area(S)[0:NE, :]
        b = banks.take()
        done = pe.transposes([(b.ap[0:NE, t * P:(t + 1) * P], gates_x[:, t, :]) for t in range(TT)], ident,
                             after=[gates_ready, b.free])
        ge_ready = evac(gates_e, b.ap[0:NE, 0:S], [done, moe0], dve)
        banks.release(b, ge_ready)

        bgu = area(2 * D)[0:NE, :]
        bdn = area(D)[0:NE, :]
        bgu_loaded = small_load("bgu_loaded", bgu, a["b_gu_2"][0], queue=pool, after=moe0)
        bdn_loaded = small_load("bdn_loaded", bdn, a["b_down_2"][0], queue=pool, after=moe0)
        fg_row = area(D)
        fg_loaded = small_load("fg_loaded", fg_row, a["final_norm_g_2"].rearrange("(o n) -> o n", o=1)
                               .broadcast_to([P, D]), queue=pool, after=moe0)

        y_acc = [banks.take() for _ in range(4)]
        done = pe.matmuls([(y_acc[2 * t + c].ap[:, :], gates_e[:, t * P:(t + 1) * P], bdn[:, c * 512:(c + 1) * 512],
                            True, False, ()) for t in range(TT) for c in range(2)],
                          after=[ge_ready, bdn_loaded, [y.free for y in y_acc]])
        bank_gate, bank_up, bank_down, bank_pick = (banks.take() for _ in range(4))

        w_gu, w_dn = a["w_gu_2"][0], a["w_down_2"][0]
        iota2 = C("iota2")
        xg_p = Pool([Buffer(area(512)) for _ in range(2)])
        sel_p = Pool([Buffer(area(512)) for _ in range(2)])
        seT_p = Pool([Buffer(area(256)) for _ in range(2)])
        glu_p = Pool([Buffer(area(3 * 512)) for _ in range(1)])
        hbT_p = Pool([Buffer(area(512)) for _ in range(1)])
        yb_p = Pool([Buffer(area(512)) for _ in range(2)])

        tbl = area(880)

        first = free_at[0]
        grown = (AREAS - first) // SLOT
        for i in range(grown):
            nb = Buffer(arena[:, first + i * SLOT:first + (i + 1) * SLOT], sem(f"slot{RING + i}_loaded"))
            nb.free = [moe0]
            ring.idle.append(nb)

        def expert_weights(src_gu, src_dn):
            gu = [unit([(lambda s: s, src_gu(k))]) for k in range(KT)]
            dn = [unit([(lambda s: s.rearrange("p (k n) -> p k n", k=2), src_dn(k))]) for k in range(KT // 2)]
            return gu, dn

        def pick(pos, gate_of, ready):
            s = sel_p.take()
            sel, selg = s.ap[:, 0:256].rearrange("p (t n) -> p t n", t=TT), s.ap[:, 256:512].rearrange("p (t n) -> p t n", t=TT)
            for t in range(TT):
                r = ts(sel[:, t, :], iota2, pos(t), ALU.is_equal, after=[ready, s.free, moe0])
                r2 = ts(selg[:, t, :], iota2, pos(t), ALU.is_equal, gate_of(t), ALU.mult, after=[ready, moe0])
            xg = xg_p.take()
            bk = bank_pick
            done = pe.matmuls([(bk.ap[:, k * CAP:(k + 1) * CAP], h_tok[:, t, k * P:(k + 1) * P], sel[:, t, 0:CAP],
                                t == 0, t == TT - 1, ()) for k in range(KT) for t in range(TT)],
                              after=[r, bk.free, htok_ready])
            xg_ready = evac(xg.ap, bk.ap[:, :], [done, xg.free, moe0], act)
            bk.free = [xg_ready]
            st = seT_p.take()
            done = pe.transposes([(bk.ap[:, t * P:(t + 1) * P], selg[:, t, :]) for t in range(TT)], ident,
                                 after=[r2, bk.free])
            st_ready = af(st.ap, bk.ap[:, 0:S], ACT.Copy, [done, st.free, moe0], scale=0.5)
            bk.free = [st_ready]
            sel_p.release(s, done)
            return xg, xg_ready, st, st_ready

        def expert_block(picked, weights, bias_row, bias_ready, between, last=False):
            xg, xg_ready, st, st_ready = picked
            gu, dn = weights
            sides = [(slice(0, CAP), 0), (slice(CAP, 2 * CAP), 512)]
            onehot = bias_row.broadcast_to([NE, CAP])
            prods = [(bk.ap[rows, :], onehot, bgu[:, c + base:c + base + 512], True, False, ())
                     for bk, base in ((bank_gate, 0), (bank_up, D)) for rows, c in sides]
            pe.matmuls(prods, after=[bank_gate.free, bank_up.free, bgu_loaded, bias_ready])
            for k in range(KT):
                lhs = xg.ap[:, k * CAP:(k + 1) * CAP]
                done = pe.matmuls([(bk.ap[rows, :], lhs, gu[k].ap[:, c + base:c + base + 512], False, k == KT - 1, ())
                                   for bk, base in ((bank_gate, 0), (bank_up, D)) for rows, c in sides],
                                  after=[gu[k].token, xg_ready])
                ring.release(gu[k], done)
            xg_p.release(xg, done)
            g = glu_p.take()
            ga, upv, th = (g.ap[:, i * 512:(i + 1) * 512] for i in range(3))
            r = ts(ga, bank_gate.ap[:, :], LIMIT, ALU.min, after=[done, g.free, moe0])
            bank_gate.free = [r]
            rt = af(th, ga, ACT.Tanh, [r, g.free], scale=ALPHA / 2)
            r = ts(upv, bank_up.ap[:, :], LIMIT, ALU.min, -LIMIT, ALU.max, after=[done, g.free])
            bank_up.free = [r]
            r = stt(upv, upv, 1.0, ga, ALU.add, ALU.mult, r)
            r = stt(upv, th, 1.0, upv, ALU.add, ALU.mult, [r, rt])
            result = between()
            done = pe.transposes([(bank_down.ap[:, j * P:(j + 1) * P], upv[:, j * P:(j + 1) * P]) for j in range(4)],
                                 ident, after=[r, bank_down.free])
            glu_p.release(g, done)
            hb = hbT_p.take()
            r = evac(hb.ap, bank_down.ap[:, :], [done, hb.free, moe0], act)
            bank_down.free = [r]
            for u in range(KT // 2):
                wv = dn[u].ap.rearrange("p (k n) -> p k n", k=2)
                prods = []
                for kk in range(2):
                    f = 2 * u + kk
                    lhs = hb.ap[:, (f % 4) * P + (f // 4) * CAP:(f % 4) * P + (f // 4 + 1) * CAP]
                    prods += [(bank_down.ap[rows, :], lhs, wv[:, kk, c:c + 512], f == 0, f == KT - 1, ())
                              for rows, c in sides]
                done = pe.matmuls(prods, after=[dn[u].token, r, bank_down.free])
                ring.release(dn[u], done)
            hbT_p.release(hb, done)
            y = yb_p.take()
            r = evac(y.ap, bank_down.ap[:, :], [done, y.free, moe0], act)
            bank_down.free = [r]

            def scatter():
                fin = pe.matmuls([(y_acc[2 * t + c].ap[:, :], st.ap[c * CAP:(c + 1) * CAP, t * P:(t + 1) * P],
                                   y.ap[c * CAP:(c + 1) * CAP, :], False, last, ()) for t in range(TT) for c in range(2)],
                                 after=[r, st_ready])
                yb_p.release(y, fin)
                seT_p.release(st, fin)
                return fin
            return result, scatter

        def pick_expert(e):
            return pick(lambda t: pos_x[:, t, e:e + 1], lambda t: gates_x[:, t, e:e + 1], [pos_ready, gates_ready])

        picked = pick_expert(0)
        scatter = None
        for e in range(NE):
            weights = expert_weights(lambda k: w_gu[e, k * P:(k + 1) * P, :],
                                     lambda k: w_dn[e, k * 256:(k + 1) * 256, :].rearrange("(k p) n -> p k n", p=P))

            def between(e=e):
                if scatter is not None:
                    scatter()
                return pick_expert(e + 1) if e + 1 < NE else None
            picked, scatter = expert_block(picked, weights, ident[0:NE, e:e + 1], const_loaded, between)
        y_done = scatter()

        outside = [(q, q.done, q.seen, q.items) for q in (pe, act, dve, sp)]
        for q, name in ((pe, "over_pe"), (act, "over_act"), (dve, "over_dve"), (sp, "over_sp")):
            q.items.append((q.waits(flag_ready), None, None, 0))
            inside = []
            q.items.append(("section", inside, flag_sb[0:1, 0:1]))
            q.items, q.done, q.seen = inside, sem(name), dict(q.seen)
        T = tbl[:, 0:64].rearrange("p (t n) -> p t n", t=TT)
        big = tbl[:, 64:128].rearrange("p (t n) -> p t n", t=TT)
        nblk, end, start = (tbl[:, 128 + i * NE:128 + (i + 1) * NE] for i in range(3))
        r = ts(nblk, cnt, float(CAP), ALU.is_gt, after=cnt_ready)
        for lim in (2 * CAP, 3 * CAP):
            r = stt(nblk, cnt, float(lim), nblk, ALU.is_gt, ALU.add, r)
        r = dve(lambda e: e.tensor_tensor_scan(end, ones[:, 0:NE], nblk, 0.0, ALU.mult, ALU.add), r)
        r = tt(start, end, nblk, ALU.subtract, r)
        r = ts(big, pos_x, float(CAP), ALU.is_ge, after=[r, pos_ready])
        r = stt(T, start.rearrange("p (o n) -> p o n", o=1).broadcast_to([P, TT, NE]), float(CAP), pos_x, ALU.mult, ALU.add, r)
        r = stt(T, T, 1.0 - CAP, big, ALU.add, ALU.mult, r)
        bk = bank_pick
        done = pe.transposes([(bk.ap[0:NE, 0:P], T[:, 0, :]), (bk.ap[0:NE, P:2 * P], T[:, 1, :]),
                              (bk.ap[0:NE, 2 * P:3 * P], start), (bk.ap[0:NE, 3 * P:4 * P], end)], ident,
                             after=[r, bk.free, y_done])
        turned = tbl[0:NE, 256:256 + 512]
        r = evac(turned, bk.ap[0:NE, :], done, dve)
        owner = tbl[0:NE, 768:768 + OVER]
        r = ts(owner, iota2[0:NE, 0:OVER], turned[:, 384:385], ALU.is_lt, after=r)
        r = stt(owner, iota2[0:NE, 0:OVER], turned[:, 256:257], owner, ALU.is_ge, ALU.mult, r)
        done = pe.matmuls([(bk.ap[:, t * OVER:(t + 1) * OVER], turned[:, t * P:(t + 1) * P], owner, True, True, ())
                           for t in range(TT)] +
                          [(bk.ap[:, (2 + t) * OVER:(3 + t) * OVER], gates_e[:, t * P:(t + 1) * P], owner, True, True, ())
                           for t in range(TT)] +
                          [(bk.ap[0:1, 4 * OVER:5 * OVER], C("part", 0, NE), owner, True, True, ())], after=r)
        bpos = tbl[:, 800:800 + 4 * OVER].rearrange("p (t n) -> p t n", n=OVER)
        r = dve(lambda e: e.tensor_copy(bpos, bk.ap[:, 0:4 * OVER].rearrange("p (t n) -> p t n", n=OVER)), done)
        for t in range(TT):
            r = stt(bpos[:, t, :], iota2[:, 0:OVER], -float(CAP), bpos[:, t, :], ALU.mult, ALU.add, r)
            r = ts(bpos[:, t, :], bpos[:, t, :], -1.0, ALU.add, after=r)
        table_ready = r
        owners_ready = dve(lambda e: e.tensor_copy(flag_sb[0:1, 1:1 + OVER], bk.ap[0:1, 4 * OVER:5 * OVER]), done)
        bk.free = [table_ready, owners_ready]
        sp.items.append((sp.waits(owners_ready), None, None, 0))
        owner_of = {}
        for n in range(OVER):
            def own(e, n=n):
                if n not in owner_of:
                    owner_of[n] = e.value_load(flag_sb[0:1, 1 + n:2 + n], min_val=0, max_val=NE - 1)
                return owner_of[n]
            weights = expert_weights(
                lambda k: (lambda e, k=k, own=own: w_gu[bass.ds(own(e), 1), k * P:(k + 1) * P, :]
                           .rearrange("o p n -> (o p) n")),
                lambda k: (lambda e, k=k, own=own: w_dn[bass.ds(own(e), 1), k * 256:(k + 1) * 256, :]
                           .rearrange("o (k p) n -> p (o k) n", p=P)))
            pk = pick(lambda t: bpos[:, t, n:n + 1], lambda t: bpos[:, 2 + t, n:n + 1], table_ready)
            _, scatter = expert_block(pk, weights, owner[:, n:n + 1], table_ready, lambda: None)
            over_done = scatter()
        dve.items.append((dve.waits(over_done), None, None, 0))
        for q, done_signal, seen, items in outside:
            q.done, q.seen, q.items = done_signal, seen, items

        y_sb = h_sb[:, :].rearrange("p (t d) -> p t d", t=TT)
        stores = []
        out_sem = sem("out_stored")
        outv = out[0].rearrange("(t p) d -> p t d", p=P)
        for t in range(TT):
            for c in range(2):
                r = tt(x_tok[:, t, c * 512:(c + 1) * 512], y_acc[2 * t + c].ap[:, :], x_tok[:, t, c * 512:(c + 1) * 512],
                       ALU.add, [y_done, xtok_ready])
            r = af(y_sb[:, t, :], x_tok[:, t, :], ACT.Square, [r, fence()], accum_out=scal[:, 8 + t:9 + t])
            r = ts(scal[:, 8 + t:9 + t], scal[:, 8 + t:9 + t], 1.0 / D, ALU.mult, EPS2, ALU.add, after=r)
            r = recip(scal[:, 8 + t:9 + t], scal[:, 8 + t:9 + t], r)
            r = af(scal[:, 8 + t:9 + t], scal[:, 8 + t:9 + t], ACT.Sqrt, r)
            r = stt(y_sb[:, t, :], x_tok[:, t, :], scal[:, 8 + t:9 + t], fg_row, ALU.mult, ALU.mult, [r, fg_loaded])
            stores.append(sp.load(out_sem, [(outv[:, t, :], y_sb[:, t, :])], after=r))
        sp.items.append((sp.waits(stores), None, None, 0))

        block = ctx.enter_context(nc.Block())

        def run(e, items):
            for item in items:
                if item[0] == "section":
                    with e.If(e.value_load(item[2], min_val=0, max_val=S) > 0):
                        run(e, item[1])
                    continue
                waits, emit, handle, amount = item
                for s, v in waits:
                    e.wait_ge(s, v)
                if emit is not None:
                    ins = emit(e)
                    if handle is not None:
                        ins.then_inc(handle, amount)

        @block.sync
        def _(e):
            run(e, sp.items)

        @block.gpsimd
        def _(e):
            run(e, pool.items)

        @block.scalar
        def _(e):
            run(e, act.items)

        @block.tensor
        def _(e):
            run(e, pe.items)

        @block.vector
        def _(e):
            run(e, dve.items)


INPUTS = ["x", "ln1_g", "w_in", "b_gate", "b_fgate", "sinks", "conv_w", "conv_b", "conv_ln_g", "conv_ln_b", "w_br",
          "w_out", "ln2_g", "w_up", "ffn_conv_w", "ffn_conv_b", "w_down", "rel_bias", "final_g", "positions_2",
          "mem_2", "attn_norm_g_2", "w_in_2", "w_pool_2", "pool_scale_2", "lambda_q1_2", "lambda_k1_2",
          "lambda_q2_2", "lambda_k2_2", "subln_g_2", "w_out_2", "xattn_norm_g_2", "mem_norm_g_2", "w_cq_2",
          "w_ckv_2", "w_co_2", "ffn_norm_g_2", "w_router_2", "b_router_2", "w_gu_2", "b_gu_2", "w_down_2",
          "b_down_2", "final_norm_g_2"]


def kernel(**inputs):
    import concourse.bacc as bacc
    from concourse.bass_utils import run_bass_kernel_spmd

    nc = bacc.Bacc("TRN2", target_bir_lowering=False, num_devices=1)
    consts, const_cols = shape_constants()
    arrays = {"in_consts": consts}
    for name in INPUTS:
        arrays["in_" + name] = np.ascontiguousarray(inputs[name])
    a = {name[3:]: nc.dram_tensor(name, v.shape, mybir.dt.from_np(v.dtype), kind="ExternalInput").ap()
         for name, v in arrays.items()}
    out = nc.dram_tensor("out", (1, S, D), F32, kind="ExternalOutput").ap()
    hybrid_moe_program(nc, a, out, const_cols)
    r = run_bass_kernel_spmd(nc, [arrays], core_ids=[0])
    return r.results[0]["out"]
```

```python
import math
from contextlib import ExitStack

import concourse.bass as bass
import numpy as np
from concourse import mybir

F32 = mybir.dt.float32
F32R = mybir.dt.float32r
I32 = mybir.dt.int32
ALU = mybir.AluOpType
ACT = mybir.ActivationFunctionType
AX = mybir.AxisListType

P = 128
S = 256
TT = S // P
D = 1024
KT = D // P
BR = D // 2
BT = BR // P
HD = 64
SWA_H, KV_H = 8, 2
SWA_WINDOW = 128
FOX_H = MOBA_H = 8
CONV_W = 31
D_FF = 2816
FT = D_FF // P
BUCKETS, MAX_DIST = 32, 128
BIAS_H = SWA_H + MOBA_H
EPS1, EPS2 = 1e-6, 1e-5
NEG = -1e30
DIFF_H, DIFF_V = 4, 128
CHUNK = 64
ROT, THETA = 16, 500000.0
LAM_INIT = 0.8 - 0.6 * math.exp(-0.3 * 0)
X_H, X_HD = 4, 256
POOL_W = (2, 4, 8, 16)
NE, TOPK = 32, 4
ALPHA, LIMIT = 1.702, 7.0
CAP = 64
OVER = S * TOPK // (CAP + 1)
TOEP = 384

SIZES = dict(qa=512, ka=128, va=128, ub=1024, qc=512, kc=512, vc=512, fc=8, qd=512, kd=512, vd=512, gz=4 * D)
OFF, _at = {}, 0
for _n, _s in SIZES.items():
    OFF[_n] = _at
    _at += _s

SLOT = 2048
RING = 4
HIGHS = 2
AREAS = 29480
SMALL = 1848


def shape_constants():
    i = np.arange(P)
    parts = {}
    parts["ident"] = np.eye(P)
    parts["flip"] = np.eye(P)[::-1]
    parts["tri"] = (i[:, None] < i[None, :])
    parts["ones"] = np.ones((P, P))
    rot = np.zeros((P, P))
    half = ROT // 2
    for head in range(P // HD):
        for d in range(half):
            rot[head * HD + half + d, head * HD + d] = -1.0
            rot[head * HD + d, head * HD + half + d] = 1.0
    parts["rot"] = rot
    freq = np.zeros((P, 1))
    base = (np.float32(THETA) ** (-np.arange(0, ROT, 2, dtype=np.float32) / np.float32(ROT))).astype(np.float32)
    for p in range(P):
        if p % HD < ROT:
            freq[p, 0] = base[(p % HD) % half]
    parts["freq"] = freq
    parts["iota2"] = np.tile(np.arange(CAP), (P, 2))
    parts["part"] = i[:, None]
    q, k = P + i[:, None], np.arange(S)[None, :]
    parts["causal"] = np.where(k <= q, 0.0, NEG)
    parts["chunk1"] = np.where(k // CHUNK <= q // CHUNK, 0.0, NEG)
    inv = np.zeros((P, 4 * 16))
    for g, w in enumerate(POOL_W):
        inv[:, g * 16:(g + 1) * 16] = 1.0 / np.minimum(np.arange(16) + 1, w)
    parts["invc"] = inv
    m = np.arange(TOEP)
    dist = 2 * P - 1 - m
    n = np.maximum(dist, 0)
    exact = BUCKETS // 2
    nf = np.maximum(n, 1).astype(np.float32)
    large = exact + (np.log(nf / np.float32(exact)) / np.float32(math.log(MAX_DIST / exact))
                     * np.float32(BUCKETS - exact)).astype(np.int32)
    bucket = np.where(n < exact, n, np.minimum(large, BUCKETS - 1))
    for name, ok in (("diag_swa", (dist >= 0) & (dist < SWA_WINDOW)), ("diag_moba", dist >= 0)):
        e = np.zeros((P, TOEP))
        e[bucket[ok], m[ok]] = 1.0
        e[BUCKETS, ~ok] = NEG
        parts[name] = e
    where, at = {}, 0
    for name, a in parts.items():
        where[name] = (at, a.shape[1])
        at += a.shape[1]
    return np.concatenate([np.asarray(a, np.float32) for a in parts.values()], axis=1), where


class Signal:

    def __init__(self, handle):
        self.handle, self.count = handle, 0


def tokens(after):
    if isinstance(after, tuple) and after and isinstance(after[0], Signal):
        return [after]
    return [t for a in after for t in tokens(a)]


class Queue:

    def __init__(self, done):
        self.done, self.items, self.seen = done, [], {}

    def waits(self, after):
        need = {}
        for s, v in tokens(after):
            if self.seen.get(s, 0) < v:
                need[s] = max(need.get(s, 0), v)
        self.seen.update(need)
        return [(s.handle, v) for s, v in need.items()]

    def __call__(self, emit, after=()):
        self.done.count += 1
        self.items.append((self.waits(after), emit, self.done.handle, 1))
        return (self.done, self.done.count)

    def matmuls(self, products, after=()):
        for n, (out, lhs, rhs, start, stop, own) in enumerate(products):
            def emit(e, out=out, lhs=lhs, rhs=rhs, start=start, stop=stop):
                return e.matmul(out, lhs, rhs, start=start, stop=stop, skip_group_check=True)
            waits = self.waits([after if n == 0 else (), own])
            last = n == len(products) - 1
            self.items.append((waits, emit, self.done.handle if last else None, 1))
        self.done.count += 1
        return (self.done, self.done.count)

    def transposes(self, pairs, ident, after=()):
        for n, (out, src) in enumerate(pairs):
            def emit(e, out=out, src=src):
                return e.transpose(out, src, ident)
            last = n == len(pairs) - 1
            self.items.append((self.waits(after if n == 0 else ()), emit, self.done.handle if last else None, 1))
        self.done.count += 1
        return (self.done, self.done.count)

    def load(self, signal, transfers, after=()):
        for n, (dst, src) in enumerate(transfers):
            def emit(e, dst=dst, src=src):
                return e.dma_start(dst, src(e) if callable(src) else src)
            self.items.append((self.waits(after if n == 0 else ()), emit, signal.handle, 16))
            signal.count += 16
        return (signal, signal.count)


class Split:

    def __init__(self, hi, lo):
        self.hi, self.lo = hi, lo

    def __getitem__(self, where):
        return Split(self.hi[where], self.lo[where])


def thrice(out, lhs, rhs, start, stop, after):
    return [(out, lhs.hi, rhs.hi, start, False, after), (out, lhs.hi, rhs.lo, False, False, ()),
            (out, lhs.lo, rhs.hi, False, stop, ())]


class Buffer:
    def __init__(self, ap, signal=None):
        self.ap, self.landed, self.free, self.held = ap, signal, [], False


class Pool:

    def __init__(self, buffers):
        self.idle = list(buffers)

    def take(self):
        b = self.idle.pop(0)
        assert not b.held
        b.held = True
        return b

    def release(self, b, readers):
        b.free, b.held = [readers], False
        self.idle.append(b)


def interleave(*stages):
    live = [iter(s) for s in stages]
    while live:
        for s in list(live):
            try:
                next(s)
            except StopIteration:
                live.remove(s)


def hybrid_moe_program(nc, a, out, const_cols):
    ctx = ExitStack()
    with ctx:
        def sem(name):
            return Signal(ctx.enter_context(nc.semaphore(name)))

        byte_at, f32r_areas = {}, {}

        def sb(name, n, parts=P, dt=F32):
            at = -(-nc.sbuf_base // 32) * 32
            t = ctx.enter_context(nc.sbuf_tensor(name, [parts, n], dt))
            byte_at[t.name], f32r_areas[t.name] = at, []
            return t

        def rounded(ap):
            t, n = ap.tensor, ap.shape[1]
            at = ap.offset % t.shape[1]
            over = nc.alloc_sbuf_tensor_at(f"{t.name}_f32r_{len(f32r_areas[t.name])}", [P, n], F32R,
                                           offset=byte_at[t.name] + 4 * at)
            f32r_areas[t.name].insert(0, (at, n, over))
            return ap

        def f32r(ap):
            part, at = divmod(ap.offset, ap.tensor.shape[1])
            first, n, over = next(r for r in f32r_areas[ap.tensor.name] if r[0] <= at < r[0] + r[1])
            return bass.AP(over, part * n + at - first, [[n, ap.ap[0][1]], *ap.ap[1:]])

        n_const = sum(w for _, w in const_cols.values())
        const_sb = sb("const_sb", n_const)
        cols_sb = sb("cols_sb", 4 * P)
        x_sb = sb("x_sb", KT * S)
        h_sb = sb("h_sb", KT * S)
        rstd_sb = sb("rstd_sb", 2 * S)
        small_sb = sb("small_sb", SMALL)
        arena_n = AREAS + (RING + HIGHS + 1) * SLOT
        arena = sb("arena", arena_n)
        flag_sb = ctx.enter_context(nc.sbuf_tensor("flag_sb", [P, 32], I32))
        pos_i = ctx.enter_context(nc.sbuf_tensor("pos_i", [P, S], I32))
        bank_t = [ctx.enter_context(nc.psum_tensor(f"bank{i}", [P, 512], F32)) for i in range(8)]
        banks = Pool([Buffer(t) for t in bank_t])
        diag_dram = nc.dram_tensor("diag_dram", (BIAS_H, TOEP), F32).ap()

        def C(name, p0=0, p1=P):
            at, w = const_cols[name]
            return const_sb[p0:p1, at:at + w]

        ident, ones = C("ident"), C("ones")

        pe, act, dve, pool = (Queue(sem(n)) for n in ("pe_done", "act_done", "dve_done", "pool_done"))
        sp = Queue(sem("sp_unused"))

        def fence():
            return [(q.done, q.done.count) for q in (pe, act, dve, pool) if q.done.count]

        def tt(o, x, y, op, after=()):
            return dve(lambda e: e.tensor_tensor(o, x, y, op), after)

        def ts(o, x, s1, op1, s2=None, op2=None, after=()):
            if op2 is None:
                return dve(lambda e: e.tensor_scalar(o, x, s1, None, op1), after)
            return dve(lambda e: e.tensor_scalar(o, x, s1, s2, op1, op2), after)

        def stt(o, x, s, y, op1, op2, after=()):
            return dve(lambda e: e.scalar_tensor_tensor(out=o, in0=x, scalar=s, in1=y, op0=op1, op1=op2), after)

        def af(o, x, f, after=(), **k):
            return act(lambda e: e.activation(o, x, f, **k), after)

        def recip(o, x, after=()):
            return dve(lambda e: e.reciprocal(o, x), after)

        def neg_max(o, x, after=()):
            return dve(lambda e: e.tensor_reduce(o, x, AX.X, ALU.max, negate=True), after)

        def evac(o, x, after, on):
            if on is act:
                return af(o, x, ACT.Copy, after)
            return dve(lambda e: e.tensor_copy(o, x), after)

        free_at = [0]

        def area(n):
            at = free_at[0]
            free_at[0] += n
            assert free_at[0] <= AREAS, free_at[0]
            return arena[:, at:at + n]

        def tiles(ap, n):
            return ap.rearrange("p (n s) -> p n s", n=n)

        def slot(i):
            return arena[:, AREAS + i * SLOT:AREAS + (i + 1) * SLOT]

        slots = [0]

        def grow(ap, free):
            b = Buffer(rounded(ap), sem(f"slot{slots[0]}_loaded"))
            b.free = free
            slots[0] += 1
            return b

        ring = Pool([grow(slot(i), []) for i in range(RING)])
        highs = Pool([Buffer(rounded(slot(RING + i))) for i in range(HIGHS)])
        h_hi = tiles(rounded(slot(RING + HIGHS)), KT)
        hi_made, lo_made = sem("hi_made"), sem("lo_made")
        ahead, depth = {}, [1]

        def split_ahead(q, made, steps):
            place, got = ahead[q][-depth[0]], []
            for n, (emit, after) in enumerate(steps):
                made.count += 1
                q.items.insert(place + n, ([(s.handle, v) for s, v in tokens(after)], emit, made.handle, 1))
                got.append((made, made.count))
            ahead[q] = [ahead[q][1] + len(steps), len(q.items)]
            return got

        def unit(transfers, split=True):
            b = ring.take()
            b.token = sp.load(b.landed, [(v(b.ap), src) for v, src in transfers], after=b.free)
            if split:
                b.high = highs.take()
                parts = [(f32r(b.high.ap[:, c:c + SLOT // 2]), f32r(b.ap[:, c:c + SLOT // 2]), b.ap[:, c:c + SLOT // 2])
                         for c in (0, SLOT // 2)]
                r = split_ahead(act, hi_made, [(lambda e, hi=hi, full=full: e.activation(hi, full, ACT.Copy),
                                                [b.token, b.high.free]) for hi, _, full in parts])
                b.halves = split_ahead(dve, lo_made, [
                    (lambda e, hi=hi, lo=lo, full=full: e.tensor_tensor(lo, full, hi, ALU.subtract), [b.token, rh])
                    for rh, (hi, lo, full) in zip(r, parts)])
            return b

        def weights_of(u, view):
            return Split(view(f32r(u.high.ap)), view(f32r(u.ap)))

        def release_unit(u, readers):
            highs.release(u.high, readers)
            ring.release(u, readers)

        def split_tile(hi, x, after, on=None):
            hi, lo = f32r(hi), f32r(x)
            r = af(hi, x, ACT.Copy, after)
            return (on or dve)(lambda e: e.tensor_tensor(lo, x, hi, ALU.subtract), [after, r])

        def both(hi, lo):
            return Split(f32r(hi), f32r(lo))

        def columns(w, c0, n=256):
            return unit([(lambda s: s[:, 0:KT * n].rearrange("p (k n) -> p k n", k=KT),
                          w[:, c0:c0 + n].rearrange("(k p) n -> p k n", p=P))])

        def small_load(name, dst, src, queue=pool, after=()):
            return queue.load(sem(name), [(dst, src)], after)

        x = tiles(x_sb[:, :], KT)
        h = tiles(rounded(h_sb[:, :]), KT)
        xin = area(2 * D).rearrange("p (t d) -> p t d", t=TT)
        first_cols = 4 * P
        first_loaded = small_load("first_loaded", const_sb[:, 0:first_cols], a["consts"][:, 0:first_cols], queue=sp)
        x_loaded = small_load("x_loaded", xin, a["x"][0].rearrange("(t p) d -> p t d", p=P), queue=sp)
        rest_loaded = small_load("rest_loaded", const_sb[:, first_cols:], a["consts"][:, first_cols:], queue=sp)
        const_loaded = [first_loaded, rest_loaded]

        rows_in = [
            [("ln1_g", a["ln1_g"][0], 8), ("b_gate", a["b_gate"][0], 32), ("conv_b", a["conv_b"][0], 4),
             ("conv_ln_g", a["conv_ln_g"][0], 4), ("conv_ln_b", a["conv_ln_b"][0], 4), ("ln2_g", a["ln2_g"][0], 8),
             ("ffn_b", a["ffn_conv_b"][0], 44), ("final_g", a["final_g"], 8)],
            [("tap0", a["ffn_conv_w"][0, 0], 44), ("tap1", a["ffn_conv_w"][0, 1], 44),
             ("attn_g", a["attn_norm_g_2"][0], 8), ("xattn_g", a["xattn_norm_g_2"][0], 8),
             ("mem_g", a["mem_norm_g_2"][0], 8), ("ffn_g", a["ffn_norm_g_2"][0], 8)],
            [("tap2", a["ffn_conv_w"][0, 2], 44), ("pool_scale", a["pool_scale_2"][0], 4),
             ("subln", a["subln_g_2"][0], 1)],
            [("conv_w", a["conv_w"][0], CONV_W * BT)],
        ]
        rows_sb = area(4 * P)
        col_at, rows_loaded = {}, []
        for t, group in enumerate(rows_in):
            r = 0
            s = sem(f"rows{t}_loaded")
            for name, src, n in group:
                flat = src if len(src.shape) == 1 else src.rearrange("a b -> (a b)")
                token = sp.load(s, [(rows_sb[r:r + n, t * P:(t + 1) * P], flat.rearrange("(r p) -> r p", p=P))])
                col_at[name] = t * P + r
                r += n
            rows_loaded.append((token, r))

        def col(name, i=0):
            return cols_sb[:, col_at[name] + i:col_at[name] + i + 1]

        sm_at = [0]

        def small(n, p1=P):
            at = sm_at[0]
            sm_at[0] += -(-n // 8) * 8
            assert sm_at[0] <= SMALL
            return small_sb[0:p1, at:at + n]

        relb = small(BIAS_H, BUCKETS + 1)
        relb_ones = dve(lambda e: e.memset(relb, 1.0))
        relb_loaded = small_load("relb_loaded", relb[0:BUCKETS, :], a["rel_bias"], after=relb_ones)
        bfg = small(1, FOX_H)
        bfg_loaded = small_load("bfg_loaded", bfg, a["b_fgate"][0].rearrange("(h o) -> h o", o=1))
        sinks = small(SWA_H)
        sinks_loaded = small_load("sinks_loaded", sinks, a["sinks"][0:1, :].broadcast_to([P, SWA_H]))
        wfc = rounded(small(KT * FOX_H)).rearrange("p (k n) -> p k n", k=KT)
        w_in = a["w_in"][0]
        wfc_loaded = small_load("wfc_loaded", wfc,
                                w_in[:, OFF["fc"]:OFF["fc"] + FOX_H].rearrange("(k p) n -> p k n", p=P))
        lams = small(4 * HD)
        lam_sem = sem("lam_loaded")
        for i, n in enumerate(("lambda_q1_2", "lambda_k1_2", "lambda_q2_2", "lambda_k2_2")):
            lam_loaded = pool.load(lam_sem, [(lams[:, i * HD:(i + 1) * HD], a[n][0:1, :].broadcast_to([P, HD]))])
        wrt = small(KT * NE).rearrange("p (k n) -> p k n", k=KT)
        wrt_loaded = small_load("wrt_loaded", wrt, a["w_router_2"][0].rearrange("(k p) n -> p k n", p=P))
        brt = small(NE)
        brt_loaded = small_load("brt_loaded", brt, a["b_router_2"][0:1, :].broadcast_to([P, NE]))
        pos_loaded = small_load("pos_loaded", pos_i[:, :], a["positions_2"][0:1, :].broadcast_to([P, S]))

        def turn(dst, src, ready):
            got = []
            for k in range(0, KT, 2):
                b = banks.take()
                done = pe.transposes([(b.ap[:, j * S + t * P:j * S + (t + 1) * P], src[:, t, (k + j) * P:(k + j + 1) * P])
                                      for j in range(2) for t in range(TT)], ident, after=[ready, first_loaded, b.free])
                got.append(evac(dst[:, k:k + 2, :], b.ap[:, :].rearrange("p (n s) -> p n s", n=2), done,
                                act if k % 4 else dve))
                banks.release(b, got[-1])
            return [got[k // 2] for k in range(KT)]

        eps_col = {}

        def inverse_root(mean, eps, done, dst):
            r = af(dst, mean, ACT.Sqrt, [done, eps_ready], bias=eps_col[eps])
            return recip(dst, dst, r)

        def sqrt_table():
            return af(spare[0:1, 0:1], ones[0:1, 0:1], ACT.Sqrt, first_loaded)

        rstd_free = [()]

        class Norm:

            def __init__(self, src, gain, eps, dst, dst_free=(), hi=None):
                self.src, self.gain, self.eps, self.dst, self.dst_free, self.hi = src, gain, eps, dst, dst_free, hi
                self.bank, self.squared, self.summed = banks.take(), [], 0

            def squares(self, k, n, ready, on=None):
                o, i = self.dst[:, k:k + n, :], self.src[:, k:k + n, :]
                if on is act or (on is None and (k // n) % 2):
                    r = af(o, i, ACT.Square, [ready, self.dst_free], scale=D ** -0.5)
                else:
                    r = stt(o, i, 1.0 / D, i, ALU.mult, ALU.mult, [ready, self.dst_free])
                self.squared += [r] * n

            def sums(self):
                new = range(self.summed, len(self.squared))
                self.done = pe.matmuls([(self.bank.ap[:, 0:S], ones, self.dst[:, k, :], k == 0, k == KT - 1,
                                         self.squared[k]) for k in new], after=[self.bank.free, first_loaded])
                self.summed = len(self.squared)

            def apply(self, out=None):
                for _ in self.steps(out):
                    pass
                return self.got

            def steps(self, out=None, on=None):
                rstd = rstd_sb[:, 0:S]
                root = inverse_root(self.bank.ap[:, 0:S], self.eps, [self.done, rstd_free[0]], rstd)
                banks.release(self.bank, root)
                self.got = got = []
                lag, dst, hi = 2, self.dst if out is None else out, self.hi
                for k in range(KT + lag):
                    if k < KT:
                        got.append(stt(dst[:, k, :], self.src[:, k, :], col(self.gain, k), rstd, ALU.mult, ALU.mult,
                                       [root, cols_ready]))
                        rstd_free[0] = got[-1]
                    if hi is not None and k >= lag:
                        got[k - lag] = split_tile(hi[:, k - lag, :], dst[:, k - lag, :],
                                                  [got[k - lag], self.dst_free], on)
                    if k % 2:
                        yield

        def project(u, act_in, ready, take, n=2):
            w = weights_of(u, lambda s: s.rearrange("p (k n) -> p k n", k=KT))
            b = banks.take()
            prods = []
            for half in (range(KT // 2), range(KT // 2, KT)):
                for j in range(n):
                    for k in half:
                        prods += thrice(b.ap[:, j * S:(j + 1) * S], w[:, k, j * P:(j + 1) * P], act_in[:, k, :],
                                        k == 0 and j == 0, k == KT - 1, [ready[k], u.halves[2 * k // KT]])
            done = pe.matmuls(prods, after=b.free)
            release_unit(u, done)
            banks.release(b, take(b.ap[:, 0:n * S].rearrange("p (n s) -> p n s", n=n), done))

        def project_tokens(u, act_in, ready, take, n=256):
            w = weights_of(u, lambda s: s.rearrange("p (k n) -> p k n", k=KT))
            b = banks.take()
            done = pe.matmuls([m for t in range(TT) for k in range(KT)
                               for m in thrice(b.ap[:, t * n:(t + 1) * n], act_in[:, k, t * P:(t + 1) * P],
                                               w[:, k, :], k == 0, k == KT - 1, [ready[k], u.halves[2 * k // KT]])],
                              after=b.free)
            release_unit(u, done)
            banks.release(b, take(b.ap[:, 0:TT * n].rearrange("p (t n) -> p t n", t=TT), done))

        x_ready = turn(x, xin, x_loaded)
        spare = small(1)
        for eps in (EPS1, EPS2):
            eps_col[eps] = small(1)
            eps_ready = dve(lambda e, eps=eps: e.memset(eps_col[eps], eps))
        norm = Norm(x, "ln1_g", EPS1, h, hi=h_hi)
        for k in range(0, KT, 2):
            norm.squares(k, 2, x_ready[k:k + 2])
        sqrt_table()
        norm.sums()
        b = banks.take()
        for t, (token, r) in enumerate(rows_loaded):
            done = pe.transposes([(b.ap[:, t * P:t * P + r], rows_sb[0:r, t * P:(t + 1) * P])], ident[0:r, 0:r],
                                 after=[token, first_loaded])
        cols_ready = []
        for t, (_, r) in enumerate(rows_loaded):
            cols_ready.append(evac(cols_sb[:, t * P:t * P + r], b.ap[:, t * P:t * P + r], done, dve))
        banks.release(b, cols_ready)
        cw0 = col_at["conv_w"]
        cols_ready.append(ts(col("subln"), col("subln"), 1.0 - LAM_INIT, ALU.mult, after=cols_ready))
        taps_ready = ts(cols_sb[:, cw0:cw0 + CONV_W * BT], cols_sb[:, cw0:cw0 + CONV_W * BT], 0.5, ALU.mult,
                        after=cols_ready)

        ahead[act], ahead[dve] = [len(act.items)] * 2, [len(dve.items)] * 2
        h_ready = norm.apply()
        hs = both(h_hi, h)
        cut_at = fence()

        yt = tiles(rounded(area(16 * S)), 16)
        gate_a = area(32 * S)
        gate = tiles(gate_a, 32)
        qkv0 = free_at[0]
        qa, qc, kc, qd, kd = (tiles(area(BT * S), BT) for _ in range(5))
        ka = area(S)
        va = area(TT * 128).rearrange("p (t n) -> p t n", t=TT)
        vc, vd = (area(TT * BR).rearrange("p (t n) -> p t n", t=TT) for _ in range(2))
        toep_a = xin.rearrange("p t d -> p (t d)")
        scores = [Buffer(area(384)) for _ in range(3)]
        probs = [Buffer(area(384)) for _ in range(3)]
        score_pool, prob_pool = Pool(scores), Pool(probs)
        fox_l, fox_rt = area(2 * S), area(2 * S)

        def fox_pair(rows, head):
            p0 = 32 * (head // 2)
            return rows[p0:p0 + 2, (head % 2) * S:(head % 2 + 1) * S]

        diag_sb = [area(TOEP)[0:n, :] for n in (SWA_H, MOBA_H)]
        b, b2 = banks.take(), banks.take()
        relb_swa = relb[:, 0:SWA_H]
        done = pe.matmuls([(b.ap[0:SWA_H, 0:TOEP], relb_swa, C("diag_swa", 0, BUCKETS + 1), True, True, ()),
                           (b2.ap[0:MOBA_H, 0:TOEP], relb[:, SWA_H:BIAS_H], C("diag_moba", 0, BUCKETS + 1), True, True, ())],
                          after=[relb_loaded, const_loaded, b.free, b2.free])
        diag_sem = sem("diag_stored")
        d1 = evac(diag_sb[0], b.ap[0:SWA_H, 0:TOEP], done, dve)
        stored = pool.load(diag_sem, [(diag_dram[0:SWA_H, :], diag_sb[0])], after=d1)
        banks.release(b, d1)
        d2 = evac(diag_sb[1], b2.ap[0:MOBA_H, 0:TOEP], done, dve)
        banks.release(b2, d2)
        stored = pool.load(diag_sem, [(diag_dram[SWA_H:BIAS_H, :], diag_sb[1])], after=d2)
        toep_pool = Pool([Buffer(toep_a[:, i * S:(i + 1) * S], sem(f"toep{i}_loaded")) for i in range(8)])

        def toeplitz(head):
            t = toep_pool.take()
            src = bass.AP(diag_dram.tensor, head * TOEP, [[1, P], [1, S]])
            t.token = pool.load(t.landed, [(t.ap, src)], after=[stored, x_ready, t.free])
            return t

        def forget_gate():
            b = banks.take()
            z = small(2 * S, FOX_H)
            zz, ez = z[:, 0:S], z[:, S:2 * S]
            wfc_hi = rounded(small(KT * FOX_H)).rearrange("p (k n) -> p k n", k=KT)
            wfc_ready = split_tile(wfc_hi, wfc, wfc_loaded)
            ws = both(wfc_hi, wfc)
            done = pe.matmuls([m for k in range(KT) for m in
                               thrice(b.ap[0:FOX_H, 0:S], ws[:, k, :], hs[:, k, :], k == 0, k == KT - 1, h_ready[k])],
                              after=[wfc_ready, b.free])
            r = ts(zz, b.ap[0:FOX_H, 0:S], bfg[:, 0:1], ALU.add, after=[done, bfg_loaded])
            banks.release(b, r)
            r = stt(ez, zz, -1.0, zz, ALU.mult, ALU.max, r)
            r = af(ez, ez, ACT.Exp, r, scale=-1.0)
            r = af(ez, ez, ACT.Ln, r, bias=1.0)
            r = stt(ez, zz, 0.0, ez, ALU.min, ALU.subtract, r)
            one = dve(lambda e: e.memset(fox_l, 1.0), cut_at)
            one2 = dve(lambda e: e.memset(fox_rt, 1.0), cut_at)
            r = dve(lambda e: e.tensor_tensor_scan(zz, ones[0:FOX_H, 0:1].broadcast_to([FOX_H, S]), ez, 0.0,
                                                   ALU.mult, ALU.add), r)
            r2 = ts(ez, zz, -1.0, ALU.mult, after=r)
            s = sem("fox_rows")
            return pool.load(s, [(fox_pair(fox_l, n)[0:1, :], zz[n:n + 1, :]) for n in range(FOX_H)] +
                             [(fox_pair(fox_rt, n)[1:2, :], ez[n:n + 1, :]) for n in range(FOX_H)],
                             after=[r, r2, one, one2])

        def keep(dst, on, scale=None, also=None):
            def take(src, done):
                if scale is not None:
                    r = af(dst, src, ACT.Copy, [done, cut_at], scale=scale) if on is act else \
                        ts(dst, src, scale, ALU.mult, after=[done, cut_at])
                else:
                    r = evac(dst, src, [done, cut_at], on)
                if also is not None:
                    also.append(r)
                return r
            return take

        made = {n: [] for n in ("qa", "ka", "va", "qc", "kc", "vc", "qd", "kd", "vd", "pad", "up", "uq", "uk", "uv")}

        def heads_qkv():
            for i in range(2):
                u = unit([(lambda s, g=g, y=y: s.rearrange("p (k y g x) -> p k y g x", k=KT, y=2, g=KV_H)[:, :, y, g, :],
                           w_in[:, (4 * g + 2 * i + y) * HD:(4 * g + 2 * i + y + 1) * HD]
                           .rearrange("(k p) x -> p k x", p=P)) for g in range(KV_H) for y in range(2)])
                project(u, hs, h_ready, keep(qa[:, 2 * i:2 * i + 2, :], act, HD ** -0.5, made["qa"]))
                yield
            u = columns(w_in, OFF["ka"])
            w = weights_of(u, lambda s: s.rearrange("p (k n) -> p k n", k=KT))
            b = banks.take()
            done = pe.matmuls([m for k in range(KT) for m in
                               thrice(b.ap[:, 0:S], w[:, k, 0:P], hs[:, k, :], k == 0, k == KT - 1,
                                      [h_ready[k], u.halves[2 * k // KT]])] +
                              [m for t in range(TT) for k in range(KT) for m in
                               thrice(b.ap[:, S + t * P:S + (t + 1) * P], hs[:, k, t * P:(t + 1) * P],
                                      w[:, k, P:2 * P], k == 0, k == KT - 1, ())],
                              after=b.free)
            release_unit(u, done)
            made["ka"].append(evac(ka, b.ap[:, 0:S], [done, cut_at], dve))
            made["va"].append(evac(va, b.ap[:, S:2 * S].rearrange("p (t n) -> p t n", t=TT),
                                   [done, cut_at, made["ka"]], act))
            banks.release(b, [made["ka"], made["va"]])
            yield
            for q, k, v, qt, kt_, vt in (("qd", "kd", "vd", qd, kd, vd), ("qc", "kc", "vc", qc, kc, vc)):
                for i in range(2):
                    project(columns(w_in, OFF[q] + i * 256), hs, h_ready,
                            keep(qt[:, 2 * i:2 * i + 2, :], act, HD ** -0.5, made[q]))
                    project(columns(w_in, OFF[k] + i * 256), hs, h_ready,
                            keep(kt_[:, 2 * i:2 * i + 2, :], dve, None, made[k]))
                    project_tokens(columns(w_in, OFF[v] + i * 256), hs, h_ready,
                                   keep(vt[:, :, i * 256:(i + 1) * 256], act, None, made[v]))
                    yield

        PARTS = (slice(0, 256), slice(256, 384))

        def softmax(bank, done, stat, sink=None):
            e = score_pool.take()
            nm, sm = stat.ap[:, 0:2], stat.ap[:, 2:4]
            for i, c in enumerate(PARTS):
                top = neg_max(nm[:, i:i + 1], bank.ap[:, c], [done, stat.free])
            if sink is not None:
                top = ts(nm, nm, neg_sinks[:, sink:sink + 1], ALU.min, after=[top, neg_ready])
            for i, c in enumerate(PARTS):
                ex = af(e.ap[:, c], bank.ap[:, c], ACT.Exp, [top, e.free, cut_at], bias=nm[:, i:i + 1],
                        accum_out=sm[:, i:i + 1])
            banks.release(bank, [top, ex])
            if sink is not None:
                es = stat.ap[:, 4:6]
                ex2 = af(es, nm, ACT.Exp, top, bias=sinks[:, sink:sink + 1])
                ex = tt(sm, sm, es, ALU.add, [ex, ex2])
            r = recip(sm, sm, ex)
            return e, r, sm

        stats = Pool([Buffer(small(6)) for _ in range(8)])

        neg_sinks = small(SWA_H)
        neg_ready = ts(neg_sinks, sinks, -1.0, ALU.mult, after=sinks_loaded)

        def attend(e, ready, values, out_ap, out_free):
            b = banks.take()
            done = pe.transposes([(b.ap[:, 0:128], e.ap[:, 256:384]), (b.ap[:, 128:256], e.ap[:, 0:128]),
                                  (b.ap[:, 256:384], e.ap[:, 128:256])], ident, after=[ready, b.free])
            score_pool.release(e, done)
            p = prob_pool.take()
            got = evac(p.ap, b.ap[:, 0:384], [done, p.free, cut_at], act)
            banks.release(b, got)
            yield
            done = pe.matmuls([(out_ap, values(0), p.ap[:, 0:256], True, False, ()),
                               (out_ap[:, 128:256], values(1), p.ap[:, 256:384], False, True, ())],
                              after=[got, out_free])
            prob_pool.release(p, done)
            yield done

        def normalize(e, r, sm):
            for i, c in enumerate(PARTS):
                r = ts(e.ap[:, c], e.ap[:, c], sm[:, i:i + 1], ALU.mult, after=r)
            return r

        def head_scores(bank, q, k, extra, after):
            prods = []
            for c, qs, ks, hs in ((PARTS[0], slice(128, 256), slice(0, 256), slice(0, 256)),
                                  (PARTS[1], slice(0, 128), slice(0, 128), slice(128, 256))):
                prods.append((bank.ap[:, c], q[:, qs], k[:, ks], True, False, ()))
                for n, (l, r) in enumerate(extra(qs, ks, hs)):
                    prods.append((bank.ap[:, c], l, r, False, n == len(extra(qs, ks, hs)) - 1, ()))
            return pe.matmuls(prods, after=[bank.free, after])

        def attention(kind):
            for pair in range(4):
                out_b = banks.take()
                dones = []
                for j in range(2):
                    stat = stats.take()
                    bank = banks.take()
                    rows = slice(j * HD, (j + 1) * HD)
                    if kind == "swa":
                        head = pair + 4 * j
                        t = toeplitz(head)
                        done = head_scores(bank, qa[rows, pair, :], ka[rows, :],
                                           lambda qs, ks, hs: [(C("flip"), t.ap[:, hs])],
                                           [made["qa"], made["ka"], t.token])
                        toep_pool.release(t, done)
                        e, r, sm = softmax(bank, done, stat, sink=head)
                        vals, dep = (lambda kb, j=j: va[:, kb, j * HD:(j + 1) * HD]), made["va"]
                    elif kind == "moba":
                        head = 2 * pair + j
                        t = toeplitz(SWA_H + head)
                        done = head_scores(bank, qd[rows, pair, :], kd[rows, pair, :],
                                           lambda qs, ks, hs: [(C("flip"), t.ap[:, hs])],
                                           [made["qd"], made["kd"], t.token])
                        toep_pool.release(t, done)
                        e, r, sm = softmax(bank, done, stat)
                        vals, dep = (lambda kb, head=head: vd[:, kb, head * HD:(head + 1) * HD]), made["vd"]
                    else:
                        head = 2 * pair + j
                        fl, fr = fox_pair(fox_l, head), fox_pair(fox_rt, head)
                        done = head_scores(bank, qc[rows, pair, :], kc[rows, pair, :],
                                           lambda qs, ks, hs: [(fl[:, qs], fr[:, ks]), (ident, C("causal")[:, hs])],
                                           [made["qc"], made["kc"], fox_ready])
                        e, r, sm = softmax(bank, done, stat)
                        vals, dep = (lambda kb, head=head: vc[:, kb, head * HD:(head + 1) * HD]), made["vc"]
                    r = normalize(e, r, sm)
                    stats.release(stat, r)
                    yield
                    for step in attend(e, [r, dep], vals, out_b.ap[rows, 0:S], out_b.free):
                        if step is None:
                            yield
                        else:
                            dones.append(step)
                    yield
                tile = {"swa": 0, "fox": 8, "moba": 12}[kind] + pair
                got = evac(yt[:, tile, :], out_b.ap[:, 0:S], [dones, cut_at], dve)
                y_ready[tile] = got
                banks.release(out_b, got)

        y_ready = [()] * 16

        PAD = CONV_W - 1
        glu = area(BT * (PAD + S)).rearrange("p (n s) -> p n s", n=BT)
        conv = tiles(area(BT * S), BT)
        tanh_pool = Pool([Buffer(area(S)) for _ in range(2)])

        def conv_input():
            zero = dve(lambda e: e.memset(glu[:, :, 0:PAD], 0.0), cut_at)
            for c in range(BT):
                u = unit([(lambda s, j=j: s[:, :].rearrange("p (k n) -> p k n", k=KT)[:, :, j * P:(j + 1) * P],
                           w_in[:, OFF["ub"] + j * BR + c * P:OFF["ub"] + j * BR + (c + 1) * P]
                           .rearrange("(k p) n -> p k n", p=P)) for j in range(2)])

                def take(src, done):
                    t = tanh_pool.take()
                    r = af(t.ap, src[:, 1, :], ACT.Tanh, [done, t.free, cut_at], scale=0.5)
                    r = stt(glu[:, c, PAD:PAD + S], t.ap, 1.0, src[:, 0, :], ALU.add, ALU.mult, [r, zero])
                    tanh_pool.release(t, r)
                    made["pad"].append(r)
                    return r
                project(u, hs, h_ready, take)
                yield

        def conv_taps():
            last = [[] for _ in range(BT)]
            for j in range(CONV_W):
                for c in range(BT):
                    w = cols_sb[:, cw0 + j * BT + c:cw0 + j * BT + c + 1]
                    if j == 0:
                        last[c] = ts(conv[:, c, :], glu[:, c, 0:S], w, ALU.mult, col("conv_b", c), ALU.add,
                                     after=[made["pad"], taps_ready, cut_at])
                    else:
                        last[c] = stt(conv[:, c, :], glu[:, c, j:j + S], w, conv[:, c, :], ALU.mult, ALU.add, last[c])
                if j % 2:
                    yield
            yield
            b = banks.take()
            done = pe.matmuls([(b.ap[:, 0:S], ones, conv[:, c, :], c == 0, c == BT - 1, last[c]) for c in range(BT)],
                              after=b.free)
            mean = rstd_sb[:, S:2 * S]
            r = ts(mean, b.ap[:, 0:S], 1.0 / BR, ALU.mult, after=done)
            sqrt_table()
            banks.release(b, r)
            r = tt(conv, conv, mean.rearrange("p (o s) -> p o s", o=1).broadcast_to([P, BT, S]), ALU.subtract, r)
            sq = glu[:, :, 0:S]
            r2 = af(sq, conv, ACT.Square, r, scale=BR ** -0.5)
            yield
            b = banks.take()
            done = pe.matmuls([(b.ap[:, 0:S], ones, sq[:, c, :], c == 0, c == BT - 1, r2) for c in range(BT)],
                              after=b.free)
            yield
            root = inverse_root(b.ap[:, 0:S], EPS1, done, mean)
            banks.release(b, root)
            yield
            r = tt(conv, conv, mean.rearrange("p (o s) -> p o s", o=1).broadcast_to([P, BT, S]), ALU.mult, root)
            for c in range(BT):
                r1 = ts(conv[:, c, :], conv[:, c, :], col("conv_ln_g", c), ALU.mult, col("conv_ln_b", c), ALU.add,
                        after=[r, cols_ready])
                r2 = af(sq[:, c, :], conv[:, c, :], ACT.Tanh, [r1, done], scale=0.5)
                r3 = ts(conv[:, c, :], conv[:, c, :], 0.5, ALU.mult, after=[r1, r2])
                y_ready[4 + c] = stt(yt[:, 4 + c, :], sq[:, c, :], 1.0, conv[:, c, :], ALU.add, ALU.mult,
                                     [r2, r3, cut_at])
                yield

        gate_ready = [()] * 32
        half_b = small(32)
        half_ready = ts(half_b, cols_sb[:, col_at["b_gate"]:col_at["b_gate"] + 32], 0.5, ALU.mult, after=cols_ready)

        def gates():
            for i in range(16):
                def take(src, done):
                    for j in range(2):
                        r = af(gate[:, 2 * i + j, :], src[:, j, :], ACT.Tanh, [done, half_ready, cut_at],
                               bias=half_b[:, 2 * i + j:2 * i + j + 1], scale=0.5)
                        gate_ready[2 * i + j] = r
                    return r
                project(columns(w_in, OFF["gz"] + i * 256), hs, h_ready, take)
                yield
                if i % 2:
                    yield

        interleave(conv_input())
        taps = conv_taps()
        for n, _ in enumerate(heads_qkv()):
            if n == 1:
                fox_ready = forget_gate()
            next(taps)
        interleave(attention("swa"), attention("moba"), attention("fox"), gates(), taps)

        free_at[0] = qkv0
        att_end = fence()
        merged = tiles(rounded(area(KT * S)), KT)
        prod_pool = Pool([Buffer(arena[:, i * 2 * S:(i + 1) * 2 * S]) for i in range(4)])
        m_ready = [()] * KT
        order = (1, 0, 3, 2)
        yt_hi = tiles(rounded(area(16 * S)), 16)
        merged_hi = tiles(rounded(area(KT * S)), KT)
        ys = both(yt_hi, yt)

        def split_branch(n):
            hi, full = yt_hi[:, BT * n:BT * (n + 1), :], yt[:, BT * n:BT * (n + 1), :]
            hi, lo = f32r(hi), f32r(full)
            r = af(hi, full, ACT.Copy, [y_ready[BT * n:BT * (n + 1)], att_end])
            r = pool(lambda e: e.tensor_tensor(lo, full, hi, ALU.subtract), r)
            y_ready[BT * n:BT * (n + 1)] = [r] * BT
        MEM0 = AREAS - 3 * SLOT
        memx_a, memt_a, memn_a = (rounded(arena[:, MEM0 + i * SLOT:MEM0 + (i + 1) * SLOT]) for i in range(3))
        memx, memt, memn = memx_a.rearrange("p (t d) -> p t d", t=TT), tiles(memt_a, KT), tiles(memn_a, KT)
        memn_hi = tiles(memx_a, KT)
        ms = both(memn_hi, memn)
        assert free_at[0] <= MEM0
        mem_loaded = small_load("mem_loaded", memx, a["mem_2"][0].rearrange("(t p) d -> p t d", p=P), queue=pool,
                                after=att_end)
        ck_ready, cv_ready = [], []

        def memory_side():
            turned = turn(memt, memx, [mem_loaded, att_end])
            yield
            norm = Norm(memt, "mem_g", EPS2, memn, att_end, memn_hi)
            for k in range(0, KT, 2):
                norm.squares(k, 2, turned[k:k + 2], on=act)
            norm.sums()
            yield
            yield from norm.steps(on=pool)
            mr = norm.got
            w = a["w_ckv_2"][0]
            for i in range(4):
                u = columns(w, i * 256)
                yield
                project(u, ms, mr, keep(ck[:, 2 * i:2 * i + 2, :], act, None, ck_ready))
                yield
            for i in range(4):
                u = columns(w, D + i * 256)
                yield
                project_tokens(u, ms, mr, keep(cv[:, :, i * 256:(i + 1) * 256], act, None, cv_ready))
                yield

        def memory_unit(between=lambda: None):
            next(memory)
            r = between()
            next(memory)
            return r
        memory = memory_side()
        split_branch(order[0])
        for at_n, n in enumerate(order):
            if at_n + 1 < len(order):
                split_branch(order[at_n + 1])
            for half in range(2):
                w_br = a["w_br"][0, n]
                cs = slice(half * 512, (half + 1) * 512)
                if n == 0:
                    wv = w_br[:, cs].rearrange("(g h d) n -> g d h n", g=KV_H, h=4)
                    u = unit([(lambda s, g=g: s[g * HD:(g + 1) * HD, :].rearrange("p (k n) -> p k n", k=BT), wv[g])
                              for g in range(KV_H)])
                else:
                    u = unit([(lambda s: s[:, :].rearrange("p (k n) -> p k n", k=BT),
                               w_br[:, cs].rearrange("(k p) n -> p k n", p=P))])
                w = weights_of(u, lambda s: s.rearrange("p (k n) -> p k n", k=BT))
                for jj in range(2):
                    b = banks.take()
                    done = pe.matmuls([m for j in range(2) for k in range(BT) for m in
                                       thrice(b.ap[:, j * S:(j + 1) * S], w[:, k, (2 * jj + j) * P:(2 * jj + j + 1) * P],
                                              ys[:, 4 * n + k, :], k == 0, k == BT - 1,
                                              [y_ready[4 * n + k], u.halves[2 * k // BT]])],
                                      after=b.free)
                    d0 = half * 4 + 2 * jj
                    g = gate[:, n * KT + d0:n * KT + d0 + 2, :]
                    src = b.ap[:, :].rearrange("p (n s) -> p n s", n=2)
                    dep = [done, gate_ready[n * KT + d0], gate_ready[n * KT + d0 + 1], att_end]
                    if n == 1:
                        r = stt(merged[:, d0:d0 + 2, :], g, 1.0, src, ALU.add, ALU.mult, dep)
                        banks.release(b, r)
                    else:
                        t = prod_pool.take()
                        tv = t.ap.rearrange("p (n s) -> p n s", n=2)
                        r = stt(tv, g, 1.0, src, ALU.add, ALU.mult, [dep, t.free])
                        banks.release(b, r)
                        sums = merged[:, d0:d0 + 2, :]
                        q = dve if n == order[-1] else pool
                        r = q(lambda e, sums=sums, tv=tv: e.tensor_tensor(sums, sums, tv, ALU.add), [r, m_ready[d0]])
                        prod_pool.release(t, r)
                    if n == order[-1]:
                        r = split_tile(merged_hi[:, d0:d0 + 2, :], merged[:, d0:d0 + 2, :], r)
                    m_ready[d0] = m_ready[d0 + 1] = r
                release_unit(u, done)
                if (at_n, half) != (len(order) - 1, 1):
                    next(memory)

        def add_residual(w, src, ready, norm, scale=None):
            got = []
            for i in range(4):
                def take(ps, done):
                    xs = x[:, 2 * i:2 * i + 2, :]
                    if scale is None:
                        r = tt(xs, ps, xs, ALU.add, done)
                    else:
                        r = stt(xs, ps, scale, xs, ALU.mult, ALU.add, done)
                    got.extend([r, r])
                    return r
                project(columns(w, i * 256), src, ready, take)
                if i:
                    norm.sums()
                norm.squares(2 * i, 2, got[-1])
            sqrt_table()
            norm.sums()
            return got

        yt_a = yt.rearrange("p n s -> p (n s)")
        ck, cv = tiles(yt_a[:, 0:KT * S], KT), yt_a[:, KT * S:].rearrange("p (t d) -> p t d", t=TT)
        cut_at = fence()
        memory_unit()

        lamv = small(4)
        lprod = small(HD)
        for i in range(2):
            r = tt(lprod, lams[:, 2 * i * HD:(2 * i + 1) * HD], lams[:, (2 * i + 1) * HD:(2 * i + 2) * HD], ALU.mult,
                   [lam_loaded, r if i else ()])
            r = dve(lambda e, i=i: e.tensor_reduce(lamv[:, i:i + 1], lprod, AX.X, ALU.add), r)
        r = af(lamv[:, 0:2], lamv[:, 0:2], ACT.Exp, r)
        r = tt(lamv[:, 2:3], lamv[:, 0:1], lamv[:, 1:2], ALU.subtract, r)
        lam_ready = ts(lamv[:, 2:3], lamv[:, 2:3], LAM_INIT, ALU.add, after=r)

        sine, cosine, turns, posf = (arena[:, i * S:(i + 1) * S] for i in range(4))
        r = dve(lambda e: e.tensor_copy(posf, pos_i[:, :]), [pos_loaded, cut_at])
        r = ts(posf, posf, C("freq"), ALU.mult, after=r)
        magic = 1.5 * 2 ** 23
        r = ts(turns, posf, 1.0 / (2 * math.pi), ALU.mult, magic, ALU.add, after=r)
        r = ts(turns, turns, magic, ALU.subtract, after=r)
        c1 = 6.28125
        c2 = float(np.float32(np.round((2 * math.pi - c1) * 2 ** 20) / 2 ** 20))
        c3 = 2 * math.pi - c1 - c2
        for c in (c1, c2, c3):
            r = stt(posf, turns, -c, posf, ALU.mult, ALU.add, r)
        rs = af(sine, posf, ACT.Sin, r)
        rc = af(cosine, posf, ACT.Sin, r, scale=0.5)
        rc = tt(cosine, cosine, cosine, ALU.mult, rc)
        rot_ready = [rs, ts(cosine, cosine, -2.0, ALU.mult, 1.0, ALU.add, after=rc)]

        norm = Norm(x, "ln2_g", EPS1, h, fence(), h_hi)
        x_ready = add_residual(a["w_out"][0], both(merged_hi, merged), m_ready, norm, scale=0.5)

        free_at[0] = qkv0
        ff_start = fence()
        cut_at = ff_start
        h_ready = memory_unit(norm.apply)
        uf_pool = Pool([Buffer(area(2 * S)) for _ in range(3)])
        th_pool = Pool([Buffer(area(S)) for _ in range(2)])
        ff, ff_hi = tiles(rounded(gate_a[:, 0:FT * S]), FT), tiles(rounded(area(FT * S)), FT)
        ffs = both(ff_hi, ff)
        ff_ready = [()] * FT
        convolved = []

        def ff_product(i, t, tv, ready):
            q = th_pool.take()
            r = af(q.ap, tv[:, 0, :], ACT.Tanh, [ready, q.free, ff_start], scale=0.5)
            r = stt(q.ap, q.ap, 1.0, tv[:, 0, :], ALU.add, ALU.mult, r)
            r = tt(ff[:, i, :], q.ap, tv[:, 1, :], ALU.mult, r)
            th_pool.release(q, r)
            uf_pool.release(t, r)
            full, hi, lo = ff[:, i, :], ffs.hi[:, i, :], ffs.lo[:, i, :]
            r = pool(lambda e: e.tensor_copy(hi, full), [r, ff_start])
            ff_ready[i] = pool(lambda e: e.tensor_tensor(lo, full, hi, ALU.subtract), r)

        w_up = a["w_up"][0]
        for i in range(FT):
            depth[0] = 2 if i > 1 else 1
            u = unit([(lambda s, j=j: s[:, :].rearrange("p (k n) -> p k n", k=KT)[:, :, j * P:(j + 1) * P],
                       w_up[:, j * D_FF + i * P:j * D_FF + (i + 1) * P].rearrange("(k p) n -> p k n", p=P))
                      for j in range(2)])

            def take(src, done):
                t = uf_pool.take()
                tv = t.ap.rearrange("p (n s) -> p n s", n=2)
                for j in range(2):
                    f = j * FT + i
                    r0 = af(tv[:, j, :], src[:, j, :], ACT.Identity, [done, t.free, ff_start, cols_ready],
                            bias=col("ffn_b", f), scale=col("tap2", f))
                r = r0
                for lag, tap in ((1, "tap1"), (2, "tap0")):
                    for j in range(2):
                        f = j * FT + i
                        r = stt(tv[:, j, lag:S], src[:, j, 0:S - lag], col(tap, f), tv[:, j, lag:S], ALU.mult, ALU.add, r)
                convolved.append((i, t, tv, r))
                return r
            project(u, hs, h_ready, take)
            if i:
                ff_product(*convolved[i - 1])
        ff_product(*convolved[-1])

        depth[0] = 1
        acc = [banks.take() for _ in range(4)]
        w_down = a["w_down"][0]
        for i in range(FT // 2):
            u = unit([(lambda s: s[:, :].rearrange("p (k n) -> p k n", k=2),
                       w_down[i * 256:(i + 1) * 256, :].rearrange("(k p) n -> p k n", p=P))])
            w = weights_of(u, lambda s: s.rearrange("p (k n) -> p k n", k=2))
            prods = []
            for kk in range(2):
                f = 2 * i + kk
                for d in range(KT):
                    prods += thrice(acc[d // 2].ap[:, (d % 2) * S:(d % 2 + 1) * S], w[:, kk, d * P:(d + 1) * P],
                                    ffs[:, f, :], f == 0 and d % 2 == 0, f == FT - 1, [ff_ready[f], u.halves[kk]])
            done = pe.matmuls(prods, after=[b.free for b in acc])
            release_unit(u, done)
        x_ready = []
        norm = Norm(x, "final_g", EPS1, h, fence())
        for j in range(4):
            r = stt(x[:, 2 * j:2 * j + 2, :], acc[j].ap[:, :].rearrange("p (n s) -> p n s", n=2), 0.5,
                    x[:, 2 * j:2 * j + 2, :], ALU.mult, ALU.add, done)
            banks.release(acc[j], r)
            norm.squares(2 * j, 2, r, on=act)

        sqrt_table()
        norm.sums()
        x_ready = memory_unit(lambda: norm.apply(out=x))

        block2 = fence()
        norm = Norm(x, "attn_g", EPS2, h, block2, h_hi)
        for k in range(0, KT, 2):
            norm.squares(k, 2, x_ready[k:k + 2], on=act)
        sqrt_table()
        norm.sums()
        h_ready = memory_unit(norm.apply)
        gate0 = free_at[0] = qkv0 - 32 * S
        up, uq, uk = (tiles(area(BT * S), BT) for _ in range(3))
        uv = area(TT * BR).rearrange("p (t n) -> p t n", t=TT)
        mix, mix_hi = (tiles(rounded(area(KT * S)), KT) for _ in range(2))
        score_pool = Pool([Buffer(area(384)) for _ in range(DIFF_H + 2)])
        prob_pool = Pool([Buffer(area(384)) for _ in range(DIFF_H)])
        cut_at = block2
        for i in (4, 5):
            ring.idle.append(grow(arena[:, AREAS - i * SLOT:AREAS - (i - 1) * SLOT], [block2]))
        assert free_at[0] <= AREAS - 5 * SLOT
        w_in2 = a["w_in_2"][0]

        def rotate(dst, i, ready):
            b = banks.take()
            done = pe.matmuls([(b.ap[:, 0:S], C("rot"), dst[:, i, :], True, True, ready)], after=b.free)
            r1 = tt(dst[:, i, :], dst[:, i, :], cosine, ALU.mult, [done, rot_ready])
            t = rot_tmp.take()
            r2 = tt(t.ap, b.ap[:, 0:S], sine, ALU.mult, [done, rot_ready, t.free])
            banks.release(b, r2)
            r = tt(dst[:, i, :], dst[:, i, :], t.ap, ALU.add, [r1, r2])
            rot_tmp.release(t, r)
            return r

        rot_tmp = Pool([Buffer(arena[:, (5 + i) * S:(6 + i) * S]) for i in range(4)])
        rotated = {"uq": [()] * BT, "uk": [()] * BT}
        for i in range(2):
            project(columns(w_in2, BR + i * 256), hs, h_ready,
                    keep(uq[:, 2 * i:2 * i + 2, :], act, HD ** -0.5, made["uq"]))
            project(columns(w_in2, 2 * BR + i * 256), hs, h_ready,
                    keep(uk[:, 2 * i:2 * i + 2, :], dve, None, made["uk"]))
            if i:
                memory_unit()
            for j in range(2 * i, 2 * i + 2):
                rotated["uq"][j] = rotate(uq, j, made["uq"][i])
                rotated["uk"][j] = rotate(uk, j, made["uk"][i])

        def values_and_pool():
            def values(i):
                project_tokens(columns(w_in2, 3 * BR + i * 256), hs, h_ready,
                               keep(uv[:, :, i * 256:(i + 1) * 256], act, None, made["uv"]))
            values(0)
            depth[0] = 2
            values(1)
            depth[0] = 1
            yield
            memory_unit()
            yield
            yield from pools

        mix_ready = [()] * KT

        def pooling():
            M = 16
            two = [arena[:, 2 * S + i * (M + S):2 * S + (i + 1) * (M + S)] for i in range(2)]
            wp = unit([(lambda s: s[:, 0:BT * P].rearrange("p (g n) -> p g n", g=BT),
                        a["w_pool_2"][0].rearrange("g p n -> p g n"))], split=False)
            wpv = wp.ap[:, 0:BT * P].rearrange("p (g n) -> p g n", g=BT)
            zero = [dve(lambda e, t=t: e.memset(t[:, 0:M], 0.0), block2) for t in two]

            def gp(o, x, y, op, after):
                return pool(lambda e: e.tensor_tensor(o, x, y, op), after)
            pooled, ready = mix_hi[:, 0:BT, :], []
            r = ()
            for g, win in enumerate(POOL_W):
                u, o = up[:, g, :], pooled[:, g, :]
                r = pool(lambda e, u=u: e.tensor_copy(two[0][:, M:M + S], u), [made["up"], zero, r])
                cur = 0
                for i in range(g + 1):
                    s, d = two[cur], two[1 - cur]
                    r = gp(d[:, M:M + S], s[:, M:M + S], s[:, M - 2 ** i:M - 2 ** i + S], ALU.add, r)
                    cur = 1 - cur
                s = two[cur]
                r = pool(lambda e, o=o, s=s, win=win: e.tensor_scalar(o, s[:, M:M + S], 1.0 / win, None, ALU.mult), r)
                r = gp(o[:, 0:M], s[:, M:2 * M], C("invc")[:, g * M:(g + 1) * M], ALU.mult, r)
                r = gp(o, o, u, ALU.subtract, r)
                ready.append(r)
            yield
            for g in range(BT):
                b = banks.take()
                done = pe.matmuls([(b.ap[:, 0:S], wpv[:, g, :], pooled[:, g, :], True, True, ())],
                                  after=[ready[g], b.free, wp.token])
                r = ts(mix[:, g, :], b.ap[:, 0:S], col("pool_scale", g), ALU.mult, after=[done, block2])
                banks.release(b, r)
                mix_ready[g] = split_tile(mix_hi[:, g, :], mix[:, g, :], [r, block2])
            yield
            ring.release(wp, done)

        def diff(head):
            maps = []
            for m in range(2):
                stat, bank = stats.take(), banks.take()
                rows = slice(m * HD, (m + 1) * HD)
                done = head_scores(bank, uq[rows, head, :], uk[rows, head, :],
                                   lambda qs, ks, hs: [(ident, C("chunk1")[:, hs])],
                                   [rotated["uq"][head], rotated["uk"][head]])
                e, r, sm = softmax(bank, done, stat)
                maps.append((e, r, sm, stat))
            (e0, r0, s0, st0), (e1, r1, s1, st1) = maps
            r = ts(s1, s1, lamv[:, 2:3], ALU.mult, after=[r1, lam_ready])
            for i, c in enumerate(PARTS):
                r = ts(e1.ap[:, c], e1.ap[:, c], s1[:, i:i + 1], ALU.mult, after=r)
                r = stt(e0.ap[:, c], e0.ap[:, c], s0[:, i:i + 1], e1.ap[:, c], ALU.mult, ALU.subtract, [r, r0])
            stats.release(st0, r)
            stats.release(st1, r)
            score_pool.release(e1, r)
            yield
            ob = banks.take()
            for step in attend(e0, [r, made["uv"][head // 2]], lambda kb: uv[:, kb, head * P:(head + 1) * P],
                               ob.ap[:, 0:S], ob.free):
                if step is None:
                    yield
                else:
                    done = step
            o = mix[:, BT + head, :]
            r = evac(o, ob.ap[:, 0:S], [done, block2], dve)
            banks.release(ob, r)
            t = rot_tmp.take()
            r2 = af(t.ap, o, ACT.Square, [r, t.free], scale=DIFF_V ** -0.5)
            yield
            b = banks.take()
            done = pe.matmuls([(b.ap[:, 0:S], ones, t.ap, True, True, ())], after=[r2, b.free])
            root = inverse_root(b.ap[:, 0:S], EPS2, done, t.ap)
            banks.release(b, root)
            r = stt(o, o, col("subln"), t.ap, ALU.mult, ALU.mult, root)
            rot_tmp.release(t, r)
            yield
            mix_ready[BT + head] = split_tile(mix_hi[:, BT + head, :], o, [r, block2])
            yield

        for i in range(2):
            project(columns(w_in2, i * 256), hs, h_ready, keep(up[:, 2 * i:2 * i + 2, :], act, None, made["up"]))
        pools = pooling()
        next(pools)
        interleave(*(diff(head) for head in range(DIFF_H)), values_and_pool())
        norm = Norm(x, "xattn_g", EPS2, h, fence(), h_hi)
        x_ready = add_residual(a["w_out_2"][0], both(mix_hi, mix), mix_ready, norm)

        h_ready = memory_unit(norm.apply)
        cq, co = memt, mix
        cq_ready, co_ready = [], [()] * KT
        before = fence()
        cut_at = before
        for i in range(4):
            project(columns(a["w_cq_2"][0], i * 256), hs, h_ready,
                    keep(cq[:, 2 * i:2 * i + 2, :], act, X_HD ** -0.5, cq_ready))
        wide = [Buffer(arena[:, gate0 + i * 512:gate0 + (i + 1) * 512]) for i in range(4)]
        es, ps = Pool(wide[0:2]), Pool(wide[2:4])

        def cross(heads):
            for head in heads:
                stat, bank, e = stats.take(), banks.take(), es.take()
                prods = []
                for t in range(TT):
                    for d in range(2):
                        f = 2 * head + d
                        prods.append((bank.ap[:, t * S:(t + 1) * S], cq[:, f, t * P:(t + 1) * P], ck[:, f, :],
                                      d == 0, d == 1, ()))
                done = pe.matmuls(prods, after=[bank.free, cq_ready, ck_ready])
                nm, sm = stat.ap[:, 0:2], stat.ap[:, 2:4]
                r = neg_max(nm, bank.ap[:, :].rearrange("p (t s) -> p t s", t=TT), [done, stat.free])
                for t in range(TT):
                    ex = af(e.ap[:, t * S:(t + 1) * S], bank.ap[:, t * S:(t + 1) * S], ACT.Exp, [r, e.free, before],
                            bias=nm[:, t:t + 1], accum_out=sm[:, t:t + 1])
                banks.release(bank, [r, ex])
                r = recip(sm, sm, ex)
                for t in range(TT):
                    r = ts(e.ap[:, t * S:(t + 1) * S], e.ap[:, t * S:(t + 1) * S], sm[:, t:t + 1], ALU.mult, after=r)
                stats.release(stat, r)
                yield
                b = banks.take()
                done = pe.transposes([(b.ap[:, kb * S + t * P:kb * S + (t + 1) * P],
                                       e.ap[:, t * S + kb * P:t * S + (kb + 1) * P])
                                      for kb in range(2) for t in range(TT)], ident, after=[r, b.free])
                es.release(e, done)
                p = ps.take()
                got = evac(p.ap, b.ap[:, :], [done, p.free, before], act)
                banks.release(b, got)
                yield
                ob = banks.take()
                done = pe.matmuls([(ob.ap[:, d * S:(d + 1) * S], cv[:, kb, head * X_HD + d * P:head * X_HD + (d + 1) * P],
                                    p.ap[:, kb * S:(kb + 1) * S], kb == 0, kb == 1, ())
                                   for d in range(2) for kb in range(2)], after=[got, ob.free, cv_ready])
                ps.release(p, done)
                r = evac(co[:, 2 * head:2 * head + 2, :], ob.ap[:, :].rearrange("p (n s) -> p n s", n=2), [done, before], dve)
                banks.release(ob, r)
                r = split_tile(mix_hi[:, 2 * head:2 * head + 2, :], co[:, 2 * head:2 * head + 2, :], [r, before])
                co_ready[2 * head] = co_ready[2 * head + 1] = r
                yield

        interleave(memory, cross((0, 2)), cross((1, 3)))
        for m in (memx_a, memn_a):
            ring.idle.append(grow(m, [fence()]))
        norm = Norm(x, "ffn_g", EPS2, h, fence())
        x_ready = add_residual(a["w_co_2"][0], both(mix_hi, co), co_ready, norm)

        h_ready = norm.apply()

        moe0 = fence()
        free_at[0] = 0
        b = banks.take()
        done = pe.matmuls([(b.ap[:, t * NE:(t + 1) * NE], h[:, k, t * P:(t + 1) * P], wrt[:, k, :],
                            k == 0, k == KT - 1, h_ready[k]) for t in range(TT) for k in range(KT)],
                          after=[b.free, wrt_loaded])

        h_tok = area(TT * D).rearrange("p (t d) -> p t d", t=TT)
        x_tok = area(TT * D).rearrange("p (t d) -> p t d", t=TT)

        def turn_back(dst, src, ready):
            got = []
            for t in range(TT):
                for q in range(2):
                    b = banks.take()
                    done = pe.transposes([(b.ap[:, j * P:(j + 1) * P], src[:, 4 * q + j, t * P:(t + 1) * P])
                                          for j in range(4)], ident, after=[ready, b.free])
                    got.append(evac(dst[:, t, q * 512:(q + 1) * 512], b.ap[:, :], [done, moe0], act))
                    banks.release(b, got[-1])
            return got
        htok_ready = turn_back(h_tok, h, h_ready)
        xtok_ready = turn_back(x_tok, x, x_ready)

        def expert_table(n=NE):
            return area(TT * n).rearrange("p (t n) -> p t n", t=TT)

        logit, mask, tmp, tmp2, gates_x, pos_x, shift_x = (expert_table() for _ in range(7))
        top8 = area(TT * 8).rearrange("p (t n) -> p t n", t=TT)
        cnt = area(NE)
        scal = area(16)
        r = tt(logit, b.ap[:, 0:TT * NE].rearrange("p (t n) -> p t n", t=TT),
               brt.rearrange("p (o n) -> p o n", o=1).broadcast_to([P, TT, NE]), ALU.add, [done, brt_loaded, moe0])
        banks.release(b, r)
        for t in range(TT):
            r0 = dve(lambda e, t=t: e.max(top8[:, t, :], logit[:, t, :]), r)
        r = r0

        def spread(columns):
            return columns.broadcast_to([P, TT, NE])
        per_token = scal[:, 0:3 * TT].rearrange("p (n t o) -> p n t o", n=3, o=1)
        left, shift, total = (per_token[:, n, :, :] for n in range(3))
        least = spread(top8[:, :, TOPK - 1:TOPK])
        shifted = tt(shift_x, logit, spread(top8[:, :, 0:1]), ALU.subtract, r)
        ex = af(gates_x, shift_x, ACT.Exp, shifted)
        r = tt(mask, logit, least, ALU.is_gt, r)
        rt = tt(tmp, logit, least, ALU.is_equal, r)
        r = dve(lambda e: e.tensor_reduce(left, mask, AX.X, ALU.add), r)
        r = ts(left, left, -1.0, ALU.mult, float(TOPK), ALU.add, after=r)
        for t in range(TT):
            rt = dve(lambda e, t=t: e.tensor_tensor_scan(tmp2[:, t, :], ones[:, 0:NE], tmp[:, t, :], 0.0, ALU.mult,
                                                         ALU.add), rt)
        r = tt(tmp2, tmp2, spread(left), ALU.is_le, [r, rt])
        r = tt(tmp, tmp2, tmp, ALU.mult, r)
        r = mask_ready = tt(mask, mask, tmp, ALU.add, r)
        r = tt(gates_x, gates_x, mask, ALU.mult, [ex, r])
        r = dve(lambda e: e.tensor_reduce(total, gates_x, AX.X, ALU.add), r)
        r = recip(total, total, r)
        r = tt(gates_x, gates_x, spread(total), ALU.mult, r)
        gates_ready = r

        b = banks.take()
        done = pe.matmuls([(b.ap[:, 0:NE], C("tri"), mask[:, 0, :], True, True, ()),
                           (b.ap[:, NE:2 * NE], C("tri"), mask[:, 1, :], True, False, ()),
                           (b.ap[:, NE:2 * NE], ones, mask[:, 0, :], False, True, ()),
                           (b.ap[:, 2 * NE:3 * NE], ones, mask[:, 0, :], True, False, ()),
                           (b.ap[:, 2 * NE:3 * NE], ones, mask[:, 1, :], False, True, ())],
                          after=[mask_ready, b.free])
        r = stt(pos_x, b.ap[:, 0:TT * NE].rearrange("p (t n) -> p t n", t=TT), 1.0, mask, ALU.add, ALU.mult, done)
        pos_ready = ts(pos_x, pos_x, -1.0, ALU.add, after=r)
        r = evac(cnt, b.ap[:, 2 * NE:3 * NE], done, dve)
        banks.release(b, [r, pos_ready])
        cnt_ready = r
        r = dve(lambda e: e.tensor_reduce(scal[:, 6:7], cnt, AX.X, ALU.max), r)
        flag_ready = ts(flag_sb[:, 0:1], scal[:, 6:7], -float(CAP), ALU.add, 0.0, ALU.max, after=r)

        gates_e = area(S)[0:NE, :]
        b = banks.take()
        done = pe.transposes([(b.ap[0:NE, t * P:(t + 1) * P], gates_x[:, t, :]) for t in range(TT)], ident,
                             after=[gates_ready, b.free])
        ge_ready = evac(gates_e, b.ap[0:NE, 0:S], [done, moe0], dve)
        banks.release(b, ge_ready)

        bgu = area(2 * D)[0:NE, :]
        bdn = area(D)[0:NE, :]
        bgu_loaded = small_load("bgu_loaded", bgu, a["b_gu_2"][0], queue=pool, after=moe0)
        bdn_loaded = small_load("bdn_loaded", bdn, a["b_down_2"][0], queue=pool, after=moe0)
        fg_row = area(D)
        fg_loaded = small_load("fg_loaded", fg_row, a["final_norm_g_2"].rearrange("(o n) -> o n", o=1)
                               .broadcast_to([P, D]), queue=pool, after=moe0)

        y_acc = [banks.take() for _ in range(4)]
        bank_gate, bank_up, bank_down, bank_pick = (banks.take() for _ in range(4))

        w_gu, w_dn = a["w_gu_2"][0], a["w_down_2"][0]
        iota2 = C("iota2")
        xg_p = Pool([Buffer(area(512)) for _ in range(2)])
        sel_p = Pool([Buffer(area(512)) for _ in range(2)])
        seT_p = Pool([Buffer(area(256)) for _ in range(2)])
        glu_p = Pool([Buffer(area(3 * 512)) for _ in range(1)])
        hbT_p = Pool([Buffer(area(512)) for _ in range(1)])
        yb_p = Pool([Buffer(area(512)) for _ in range(2)])

        tbl = area(880)

        for b in highs.idle:
            ring.idle.append(grow(b.ap, b.free))
        ring.idle.append(grow(slot(RING + HIGHS), [moe0]))
        ring.idle.append(grow(memt_a, [moe0]))
        for i in range(6, (AREAS - free_at[0]) // SLOT + 1):
            ring.idle.append(grow(arena[:, AREAS - i * SLOT:AREAS - (i - 1) * SLOT], [moe0]))

        def expert_weights(src_gu, src_dn):
            gu = [unit([(lambda s: s, src_gu(k))], split=False) for k in range(KT)]
            dn = [unit([(lambda s: s.rearrange("p (k n) -> p k n", k=2), src_dn(k))], split=False) for k in range(KT // 2)]
            return gu, dn

        def pick(pos, gate_of, ready):
            s = sel_p.take()
            sel, selg = s.ap[:, 0:256].rearrange("p (t n) -> p t n", t=TT), s.ap[:, 256:512].rearrange("p (t n) -> p t n", t=TT)
            for t in range(TT):
                r = ts(sel[:, t, :], iota2, pos(t), ALU.is_equal, after=[ready, s.free, moe0])
                r2 = ts(selg[:, t, :], iota2, pos(t), ALU.is_equal, gate_of(t), ALU.mult, after=[ready, moe0])
            xg = xg_p.take()
            bk = bank_pick
            done = pe.matmuls([(bk.ap[:, k * CAP:(k + 1) * CAP], h_tok[:, t, k * P:(k + 1) * P], sel[:, t, 0:CAP],
                                t == 0, t == TT - 1, ()) for k in range(KT) for t in range(TT)],
                              after=[r, bk.free, htok_ready])
            xg_ready = evac(xg.ap, bk.ap[:, :], [done, xg.free, moe0], act)
            bk.free = [xg_ready]
            st = seT_p.take()
            done = pe.transposes([(bk.ap[:, t * P:(t + 1) * P], selg[:, t, :]) for t in range(TT)], ident,
                                 after=[r2, bk.free])
            st_ready = af(st.ap, bk.ap[:, 0:S], ACT.Copy, [done, st.free, moe0], scale=0.5)
            bk.free = [st_ready]
            sel_p.release(s, done)
            return xg, xg_ready, st, st_ready

        def expert_block(picked, weights, bias_row, bias_ready, between, last=False):
            xg, xg_ready, st, st_ready = picked
            gu, dn = weights
            sides = [(slice(0, CAP), 0), (slice(CAP, 2 * CAP), 512)]
            onehot = bias_row.broadcast_to([NE, CAP])
            prods = [(bk.ap[rows, :], onehot, bgu[:, c + base:c + base + 512], True, False, ())
                     for bk, base in ((bank_gate, 0), (bank_up, D)) for rows, c in sides]
            pe.matmuls(prods, after=[bank_gate.free, bank_up.free, bgu_loaded, bias_ready])
            for k in range(KT):
                lhs = xg.ap[:, k * CAP:(k + 1) * CAP]
                done = pe.matmuls([(bk.ap[rows, :], lhs, gu[k].ap[:, c + base:c + base + 512], False, k == KT - 1, ())
                                   for bk, base in ((bank_gate, 0), (bank_up, D)) for rows, c in sides],
                                  after=[gu[k].token, xg_ready])
                ring.release(gu[k], done)
            xg_p.release(xg, done)
            g = glu_p.take()
            ga, upv, th = (g.ap[:, i * 512:(i + 1) * 512] for i in range(3))
            r = ts(ga, bank_gate.ap[:, :], LIMIT, ALU.min, after=[done, g.free, moe0])
            bank_gate.free = [r]
            rt = af(th, ga, ACT.Tanh, [r, g.free], scale=ALPHA / 2)
            r = ts(upv, bank_up.ap[:, :], LIMIT, ALU.min, -LIMIT, ALU.max, after=[done, g.free])
            bank_up.free = [r]
            r = stt(upv, upv, 1.0, ga, ALU.add, ALU.mult, r)
            r = stt(upv, th, 1.0, upv, ALU.add, ALU.mult, [r, rt])
            result = between()
            done = pe.transposes([(bank_down.ap[:, j * P:(j + 1) * P], upv[:, j * P:(j + 1) * P]) for j in range(4)],
                                 ident, after=[r, bank_down.free])
            glu_p.release(g, done)
            hb = hbT_p.take()
            r = evac(hb.ap, bank_down.ap[:, :], [done, hb.free, moe0], act)
            bank_down.free = [r]
            for u in range(KT // 2):
                wv = dn[u].ap.rearrange("p (k n) -> p k n", k=2)
                prods = []
                for kk in range(2):
                    f = 2 * u + kk
                    lhs = hb.ap[:, (f % 4) * P + (f // 4) * CAP:(f % 4) * P + (f // 4 + 1) * CAP]
                    prods += [(bank_down.ap[rows, :], lhs, wv[:, kk, c:c + 512], f == 0, f == KT - 1, ())
                              for rows, c in sides]
                done = pe.matmuls(prods, after=[dn[u].token, r, bank_down.free])
                ring.release(dn[u], done)
            hbT_p.release(hb, done)
            y = yb_p.take()
            r = evac(y.ap, bank_down.ap[:, :], [done, y.free, moe0], act)
            bank_down.free = [r]

            def scatter():
                fin = pe.matmuls([(y_acc[2 * t + c].ap[:, :], st.ap[c * CAP:(c + 1) * CAP, t * P:(t + 1) * P],
                                   y.ap[c * CAP:(c + 1) * CAP, :], False, last, ()) for t in range(TT) for c in range(2)],
                                 after=[r, st_ready])
                yb_p.release(y, fin)
                seT_p.release(st, fin)
                return fin
            return result, scatter

        def pick_expert(e):
            return pick(lambda t: pos_x[:, t, e:e + 1], lambda t: gates_x[:, t, e:e + 1], [pos_ready, gates_ready])

        picked = pick_expert(0)
        scatter = None
        for e in range(NE):
            weights = expert_weights(lambda k: w_gu[e, k * P:(k + 1) * P, :],
                                     lambda k: w_dn[e, k * 256:(k + 1) * 256, :].rearrange("(k p) n -> p k n", p=P))

            def between(e=e):
                if scatter is not None:
                    scatter()
                else:
                    pe.matmuls([(y_acc[2 * t + c].ap[:, :], gates_e[:, t * P:(t + 1) * P],
                                 bdn[:, c * 512:(c + 1) * 512], True, False, ()) for t in range(TT) for c in range(2)],
                               after=[ge_ready, bdn_loaded, [y.free for y in y_acc]])
                return pick_expert(e + 1) if e + 1 < NE else None
            picked, scatter = expert_block(picked, weights, ident[0:NE, e:e + 1], const_loaded, between)
        y_done = scatter()

        outside = [(q, q.done, q.seen, q.items) for q in (pe, act, dve, sp)]
        for q, name in ((pe, "over_pe"), (act, "over_act"), (dve, "over_dve"), (sp, "over_sp")):
            q.items.append((q.waits(flag_ready), None, None, 0))
            inside = []
            q.items.append(("section", inside, flag_sb[0:1, 0:1]))
            q.items, q.done, q.seen = inside, sem(name), dict(q.seen)
        T = tbl[:, 0:64].rearrange("p (t n) -> p t n", t=TT)
        big = tbl[:, 64:128].rearrange("p (t n) -> p t n", t=TT)
        nblk, end, start = (tbl[:, 128 + i * NE:128 + (i + 1) * NE] for i in range(3))
        r = ts(nblk, cnt, float(CAP), ALU.is_gt, after=cnt_ready)
        for lim in (2 * CAP, 3 * CAP):
            r = stt(nblk, cnt, float(lim), nblk, ALU.is_gt, ALU.add, r)
        r = dve(lambda e: e.tensor_tensor_scan(end, ones[:, 0:NE], nblk, 0.0, ALU.mult, ALU.add), r)
        r = tt(start, end, nblk, ALU.subtract, r)
        r = ts(big, pos_x, float(CAP), ALU.is_ge, after=[r, pos_ready])
        r = stt(T, start.rearrange("p (o n) -> p o n", o=1).broadcast_to([P, TT, NE]), float(CAP), pos_x, ALU.mult, ALU.add, r)
        r = stt(T, T, 1.0 - CAP, big, ALU.add, ALU.mult, r)
        bk = bank_pick
        done = pe.transposes([(bk.ap[0:NE, 0:P], T[:, 0, :]), (bk.ap[0:NE, P:2 * P], T[:, 1, :]),
                              (bk.ap[0:NE, 2 * P:3 * P], start), (bk.ap[0:NE, 3 * P:4 * P], end)], ident,
                             after=[r, bk.free, y_done])
        turned = tbl[0:NE, 256:256 + 512]
        r = evac(turned, bk.ap[0:NE, :], done, dve)
        owner = tbl[0:NE, 768:768 + OVER]
        r = ts(owner, iota2[0:NE, 0:OVER], turned[:, 384:385], ALU.is_lt, after=r)
        r = stt(owner, iota2[0:NE, 0:OVER], turned[:, 256:257], owner, ALU.is_ge, ALU.mult, r)
        done = pe.matmuls([(bk.ap[:, t * OVER:(t + 1) * OVER], turned[:, t * P:(t + 1) * P], owner, True, True, ())
                           for t in range(TT)] +
                          [(bk.ap[:, (2 + t) * OVER:(3 + t) * OVER], gates_e[:, t * P:(t + 1) * P], owner, True, True, ())
                           for t in range(TT)] +
                          [(bk.ap[0:1, 4 * OVER:5 * OVER], C("part", 0, NE), owner, True, True, ())], after=r)
        bpos = tbl[:, 800:800 + 4 * OVER].rearrange("p (t n) -> p t n", n=OVER)
        r = dve(lambda e: e.tensor_copy(bpos, bk.ap[:, 0:4 * OVER].rearrange("p (t n) -> p t n", n=OVER)), done)
        for t in range(TT):
            r = stt(bpos[:, t, :], iota2[:, 0:OVER], -float(CAP), bpos[:, t, :], ALU.mult, ALU.add, r)
            r = ts(bpos[:, t, :], bpos[:, t, :], -1.0, ALU.add, after=r)
        table_ready = r
        owners_ready = dve(lambda e: e.tensor_copy(flag_sb[0:1, 1:1 + OVER], bk.ap[0:1, 4 * OVER:5 * OVER]), done)
        bk.free = [table_ready, owners_ready]
        sp.items.append((sp.waits(owners_ready), None, None, 0))
        owner_of = {}
        for n in range(OVER):
            def own(e, n=n):
                if n not in owner_of:
                    owner_of[n] = e.value_load(flag_sb[0:1, 1 + n:2 + n], min_val=0, max_val=NE - 1)
                return owner_of[n]
            weights = expert_weights(
                lambda k: (lambda e, k=k, own=own: w_gu[bass.ds(own(e), 1), k * P:(k + 1) * P, :]
                           .rearrange("o p n -> (o p) n")),
                lambda k: (lambda e, k=k, own=own: w_dn[bass.ds(own(e), 1), k * 256:(k + 1) * 256, :]
                           .rearrange("o (k p) n -> p (o k) n", p=P)))
            pk = pick(lambda t: bpos[:, t, n:n + 1], lambda t: bpos[:, 2 + t, n:n + 1], table_ready)
            _, scatter = expert_block(pk, weights, owner[:, n:n + 1], table_ready, lambda: None)
            over_done = scatter()
        dve.items.append((dve.waits(over_done), None, None, 0))
        for q, done_signal, seen, items in outside:
            q.done, q.seen, q.items = done_signal, seen, items

        y_sb = h_sb[:, :].rearrange("p (t d) -> p t d", t=TT)
        stores = []
        out_sem = sem("out_stored")
        outv = out[0].rearrange("(t p) d -> p t d", p=P)
        squared = []
        for t in range(TT):
            for c in range(2):
                r = tt(x_tok[:, t, c * 512:(c + 1) * 512], y_acc[2 * t + c].ap[:, :], x_tok[:, t, c * 512:(c + 1) * 512],
                       ALU.add, [y_done, xtok_ready])
            squared.append(af(y_sb[:, t, :], x_tok[:, t, :], ACT.Square, [r, fence()], accum_out=scal[:, 8 + t:9 + t],
                              scale=D ** -0.5))
        for t in range(TT):
            root = scal[:, 8 + t:9 + t]
            r = recip(root, root, af(root, root, ACT.Sqrt, squared[t], bias=eps_col[EPS2]))
            r = stt(y_sb[:, t, :], x_tok[:, t, :], root, fg_row, ALU.mult, ALU.mult, [r, fg_loaded])
            stores.append(sp.load(out_sem, [(outv[:, t, :], y_sb[:, t, :])], after=r))
        sp.items.append((sp.waits(stores), None, None, 0))

        block = ctx.enter_context(nc.Block())

        def run(e, items):
            for item in items:
                if item[0] == "section":
                    with e.If(e.value_load(item[2], min_val=0, max_val=S) > 0):
                        run(e, item[1])
                    continue
                waits, emit, handle, amount = item
                for s, v in waits:
                    e.wait_ge(s, v)
                if emit is not None:
                    ins = emit(e)
                    if handle is not None:
                        ins.then_inc(handle, amount)

        @block.sync
        def _(e):
            run(e, sp.items)

        @block.gpsimd
        def _(e):
            run(e, pool.items)

        @block.scalar
        def _(e):
            run(e, act.items)

        @block.tensor
        def _(e):
            run(e, pe.items)

        @block.vector
        def _(e):
            run(e, dve.items)


INPUTS = ["x", "ln1_g", "w_in", "b_gate", "b_fgate", "sinks", "conv_w", "conv_b", "conv_ln_g", "conv_ln_b", "w_br",
          "w_out", "ln2_g", "w_up", "ffn_conv_w", "ffn_conv_b", "w_down", "rel_bias", "final_g", "positions_2",
          "mem_2", "attn_norm_g_2", "w_in_2", "w_pool_2", "pool_scale_2", "lambda_q1_2", "lambda_k1_2",
          "lambda_q2_2", "lambda_k2_2", "subln_g_2", "w_out_2", "xattn_norm_g_2", "mem_norm_g_2", "w_cq_2",
          "w_ckv_2", "w_co_2", "ffn_norm_g_2", "w_router_2", "b_router_2", "w_gu_2", "b_gu_2", "w_down_2",
          "b_down_2", "final_norm_g_2"]


def kernel(**inputs):
    import concourse.bacc as bacc
    from concourse.bass_utils import run_bass_kernel_spmd

    nc = bacc.Bacc("TRN2", target_bir_lowering=False, num_devices=1)
    consts, const_cols = shape_constants()
    arrays = {"in_consts": consts}
    for name in INPUTS:
        arrays["in_" + name] = np.ascontiguousarray(inputs[name])
    a = {name[3:]: nc.dram_tensor(name, v.shape, mybir.dt.from_np(v.dtype), kind="ExternalInput").ap()
         for name, v in arrays.items()}
    out = nc.dram_tensor("out", (1, S, D), F32, kind="ExternalOutput").ap()
    hybrid_moe_program(nc, a, out, const_cols)
    r = run_bass_kernel_spmd(nc, [arrays], core_ids=[0])
    return r.results[0]["out"]
```
